# Optimizing a Trainium2 kernel written in Bass

```python
import math
import jax, jax.numpy as jnp
from jax import lax
import numpy as np

D_MODEL = 1024
BATCH = 1
SEQ = 256
DEPTH = 2

N_A_LAYERS = DEPTH // 2
N_B_LAYERS = DEPTH - N_A_LAYERS

A_HEADS = 4
A_QK_DIM = D_MODEL // 2 // A_HEADS
A_V_DIM = D_MODEL // A_HEADS
A_CHUNK = 64
GATE_SOFTCAP = 15.0
A_IN_DIM = 2 * A_HEADS * A_QK_DIM + 2 * A_HEADS * A_V_DIM + 2 * A_HEADS

B_GROUPS = ((128, 1), (512, 4), (2048, 16))
N_GROUPS = len(B_GROUPS)
B_HEAD_DIM = 64
B_HEADS = D_MODEL // B_HEAD_DIM
B_BLOCK = 128
REL_BUCKETS = 32
REL_MAX_DIST = 2048

D_FF = 2816
CONV_WIDTH = 3
EPS = 1e-6

kernel_name = "yoco_mlstm_dilated_attn_convffn"

def rmsnorm(x, g):
    xf = x.astype(jnp.float32)
    y = xf * lax.rsqrt(jnp.mean(xf * xf, axis=-1, keepdims=True) + EPS)
    return (y * g.astype(jnp.float32)).astype(x.dtype)

def softcap(z):
    return GATE_SOFTCAP * jnp.tanh(z / GATE_SOFTCAP)

def mlstm_chunkwise(q, k, v, li, lf):
    Bsz, S, H, dk = q.shape
    dv = v.shape[-1]
    L = A_CHUNK
    NC = S // L

    def to_chunks(t):
        return t.reshape(Bsz, NC, L, H, t.shape[-1]).transpose(1, 0, 3, 2, 4)

    def gate_chunks(t):
        return t.reshape(Bsz, NC, L, H).transpose(1, 0, 3, 2)

    causal = jnp.tril(jnp.ones((L, L), dtype=bool))

    def step(carry, xs):
        C, n, m = carry
        qc, kc, vc, lic, lfc = xs
        b = jnp.cumsum(lfc, axis=-1)
        logD = b[..., :, None] - b[..., None, :] + lic[..., None, :]
        logD = jnp.where(causal, logD, -jnp.inf)
        m_inter = b + m[..., None]
        m_t = jnp.maximum(m_inter, jnp.max(logD, axis=-1))
        Sm = jnp.einsum('bhtd,bhsd->bhts', qc, kc) * jnp.exp(logD - m_t[..., None])
        w_inter = jnp.exp(m_inter - m_t)
        num = (jnp.einsum('bhts,bhsv->bhtv', Sm, vc)
               + w_inter[..., None] * jnp.einsum('bhtd,bhdv->bhtv', qc, C))
        den = jnp.sum(Sm, axis=-1) + w_inter * jnp.einsum('bhtd,bhd->bht', qc, n)
        h = num / jnp.maximum(jnp.abs(den), jnp.exp(-m_t))[..., None]
        bL = b[..., -1]
        g = bL[..., None] - b + lic
        m_new = jnp.maximum(bL + m, jnp.max(g, axis=-1))
        wk = jnp.exp(g - m_new[..., None])
        decay = jnp.exp(bL + m - m_new)
        C_new = decay[..., None, None] * C + jnp.einsum('bhs,bhsd,bhsv->bhdv', wk, kc, vc)
        n_new = decay[..., None] * n + jnp.einsum('bhs,bhsd->bhd', wk, kc)
        return (C_new, n_new, m_new), h

    init = (jnp.zeros((Bsz, H, dk, dv), jnp.float32),
            jnp.zeros((Bsz, H, dk), jnp.float32),
            jnp.zeros((Bsz, H), jnp.float32))
    _, hs = lax.scan(step, init, (to_chunks(q), to_chunks(k), to_chunks(v),
                                  gate_chunks(li), gate_chunks(lf)))
    return hs.transpose(1, 0, 3, 2, 4).reshape(Bsz, S, H, dv)

def mlstm_layer(x, norm_g, w_in, b_if, hnorm_g, w_out):
    Bsz, S, _ = x.shape
    nq = A_HEADS * A_QK_DIM
    nv = A_HEADS * A_V_DIM
    z = rmsnorm(x, norm_g) @ w_in
    q, k, v, o, gi, gf = jnp.split(
        z, [nq, 2 * nq, 2 * nq + nv, 2 * nq + 2 * nv, 2 * nq + 2 * nv + A_HEADS], axis=-1)
    q = q.reshape(Bsz, S, A_HEADS, A_QK_DIM).astype(jnp.float32) * (A_QK_DIM ** -0.5)
    k = k.reshape(Bsz, S, A_HEADS, A_QK_DIM).astype(jnp.float32)
    v = v.reshape(Bsz, S, A_HEADS, A_V_DIM).astype(jnp.float32)
    bf = b_if.astype(jnp.float32)
    li = softcap(gi.astype(jnp.float32) + bf[:A_HEADS])
    lf = jax.nn.log_sigmoid(softcap(gf.astype(jnp.float32) + bf[A_HEADS:]))
    h = mlstm_chunkwise(q, k, v, li, lf)
    h = h * lax.rsqrt(jnp.mean(h * h, axis=-1, keepdims=True) + EPS) * hnorm_g.astype(jnp.float32)
    h = h.astype(x.dtype) * jax.nn.sigmoid(o.reshape(Bsz, S, A_HEADS, A_V_DIM))
    return h.reshape(Bsz, S, nv) @ w_out

def conv_ffn(x, norm_g, w_up, conv_w, conv_b, w_down):
    u = rmsnorm(x, norm_g) @ w_up
    up = jnp.pad(u, ((0, 0), (CONV_WIDTH - 1, 0), (0, 0)))
    u = up[:, :-2] * conv_w[0] + up[:, 1:-1] * conv_w[1] + up[:, 2:] * conv_w[2] + conv_b
    gate, val = jnp.split(u, 2, axis=-1)
    return (jax.nn.silu(gate) * val) @ w_down

def t5_bucket(dist):
    max_exact = REL_BUCKETS // 2
    d = np.maximum(dist, 0)
    log_ratio = np.log(np.maximum(d, 1) / max_exact) / math.log(REL_MAX_DIST / max_exact)
    large = np.minimum(max_exact + (log_ratio * (REL_BUCKETS - max_exact)).astype(np.int64),
                       REL_BUCKETS - 1)
    return np.where(d < max_exact, d, large).astype(np.int32)

def dilated_group(q, k, v, bias, win, dil):
    Bsz, S_pad, H, dh = q.shape
    nb = S_pad // (dil * B_BLOCK)

    def blocks(t):
        return t.reshape(Bsz, nb, B_BLOCK, dil, H, dh)

    def with_prev(t):
        prev = jnp.pad(t[:, :-1], ((0, 0), (1, 0), (0, 0), (0, 0), (0, 0), (0, 0)))
        return jnp.concatenate([prev, t], axis=2)

    qb = blocks(q)
    kc, vc = with_prev(blocks(k)), with_prev(blocks(v))
    delta = B_BLOCK + np.arange(B_BLOCK)[:, None] - np.arange(2 * B_BLOCK)[None, :]
    band = (delta >= 0) & (delta <= win // dil)
    first = (np.arange(nb)[:, None, None] == 0) & (np.arange(2 * B_BLOCK)[None, None, :] < B_BLOCK)
    valid = jnp.asarray(band[None] & ~first)[None, :, None, None]
    s = jnp.einsum('bnqrhe,bnkrhe->bnrhqk', qb, kc).astype(jnp.float32) * (dh ** -0.5) + bias
    s = jnp.where(valid, s, -jnp.inf)
    m = jnp.max(s, axis=-1, keepdims=True)
    p = jnp.exp(s - m)
    l = jnp.sum(p, axis=-1)
    o = jnp.einsum('bnrhqk,bnkrhe->bnrhqe', p.astype(vc.dtype), vc).astype(jnp.float32) / l[..., None]
    lse = m[..., 0] + jnp.log(l)
    o = o.transpose(0, 1, 4, 2, 3, 5).reshape(Bsz, S_pad, H, dh)
    lse = lse.transpose(0, 1, 4, 2, 3).reshape(Bsz, S_pad, H)
    return o, lse

def dilated_attention_layer(x, k_sh, v_sh, norm_g, w_q, w_out, rel_bias):
    Bsz, S, _ = x.shape
    q = (rmsnorm(x, norm_g) @ w_q).reshape(Bsz, S, N_GROUPS, B_HEADS, B_HEAD_DIM)
    span = max(d for _, d in B_GROUPS) * B_BLOCK
    S_pad = -(-S // span) * span
    padw = ((0, 0), (0, S_pad - S), (0, 0), (0, 0), (0, 0))
    q, k, v = jnp.pad(q, padw), jnp.pad(k_sh, padw), jnp.pad(v_sh, padw)
    outs, lses = [], []
    for g, (win, dil) in enumerate(B_GROUPS):
        delta = B_BLOCK + np.arange(B_BLOCK)[:, None] - np.arange(2 * B_BLOCK)[None, :]
        bucket = t5_bucket(delta * dil)
        bias = rel_bias[bucket][..., g * B_HEADS:(g + 1) * B_HEADS]
        bias = bias.transpose(2, 0, 1).astype(jnp.float32)
        o, lse = dilated_group(q[:, :, g], k[:, :, g], v[:, :, g], bias, win, dil)
        outs.append(o)
        lses.append(lse)
    w = jax.nn.softmax(jnp.stack(lses), axis=0)
    out = jnp.sum(w[..., None] * jnp.stack(outs), axis=0)[:, :S]
    return out.astype(x.dtype).reshape(Bsz, S, B_HEADS * B_HEAD_DIM) @ w_out

def shared_kv(x, kv_norm_g, w_kv):
    Bsz, S, _ = x.shape
    kv = (rmsnorm(x, kv_norm_g) @ w_kv).reshape(Bsz, S, 2, N_GROUPS, B_HEADS, B_HEAD_DIM)
    return kv[:, :, 0], kv[:, :, 1]

def setup_inputs(seed: int = 0) -> dict:
    key = jax.random.key(seed)
    ks = jax.random.split(key, 20)
    f32 = jnp.float32
    nrm = lambda k, s, sc: jax.random.normal(k, s, f32) * sc
    att_w = N_GROUPS * B_HEADS * B_HEAD_DIM
    return {
        "x": nrm(ks[0], (BATCH, SEQ, D_MODEL), 1.0),
        "a_norm_g": 1.0 + nrm(ks[1], (N_A_LAYERS, D_MODEL), 0.02),
        "a_w_in": nrm(ks[2], (N_A_LAYERS, D_MODEL, A_IN_DIM), D_MODEL ** -0.5),
        "a_b_if": jnp.concatenate([nrm(ks[3], (N_A_LAYERS, A_HEADS), 0.1),
                                   3.0 + 3.0 * jax.random.uniform(ks[4], (N_A_LAYERS, A_HEADS), f32)], axis=-1),
        "a_hnorm_g": 1.0 + nrm(ks[5], (N_A_LAYERS, A_HEADS, A_V_DIM), 0.02),
        "a_w_out": nrm(ks[6], (N_A_LAYERS, A_HEADS * A_V_DIM, D_MODEL), (A_HEADS * A_V_DIM) ** -0.5),
        "kv_norm_g": 1.0 + nrm(ks[7], (D_MODEL,), 0.02),
        "w_kv": nrm(ks[8], (D_MODEL, 2 * att_w), D_MODEL ** -0.5),
        "b_norm_g": 1.0 + nrm(ks[9], (N_B_LAYERS, D_MODEL), 0.02),
        "b_w_q": nrm(ks[10], (N_B_LAYERS, D_MODEL, att_w), D_MODEL ** -0.5),
        "b_w_out": nrm(ks[11], (N_B_LAYERS, B_HEADS * B_HEAD_DIM, D_MODEL), (B_HEADS * B_HEAD_DIM) ** -0.5),
        "rel_bias": nrm(ks[12], (REL_BUCKETS, N_GROUPS * B_HEADS), 0.5),
        "f_norm_g": 1.0 + nrm(ks[13], (DEPTH, D_MODEL), 0.02),
        "f_w_up": nrm(ks[14], (DEPTH, D_MODEL, 2 * D_FF), D_MODEL ** -0.5),
        "f_conv_w": nrm(ks[15], (DEPTH, CONV_WIDTH, 2 * D_FF), CONV_WIDTH ** -0.5),
        "f_conv_b": nrm(ks[16], (DEPTH, 2 * D_FF), 0.01),
        "f_w_down": nrm(ks[17], (DEPTH, D_FF, D_MODEL), D_FF ** -0.5),
        "final_norm_g": 1.0 + nrm(ks[18], (D_MODEL,), 0.02),
    }

def reference(x, a_norm_g, a_w_in, a_b_if, a_hnorm_g, a_w_out, kv_norm_g, w_kv,
              b_norm_g, b_w_q, b_w_out, rel_bias, f_norm_g, f_w_up, f_conv_w,
              f_conv_b, f_w_down, final_norm_g):
    k_sh = v_sh = None
    for layer in range(DEPTH):
        if layer < N_A_LAYERS:
            x = x + mlstm_layer(x, a_norm_g[layer], a_w_in[layer], a_b_if[layer],
                                a_hnorm_g[layer], a_w_out[layer])
        else:
            j = layer - N_A_LAYERS
            if j == 0:
                k_sh, v_sh = shared_kv(x, kv_norm_g, w_kv)
            x = x + dilated_attention_layer(x, k_sh, v_sh, b_norm_g[j], b_w_q[j],
                                            b_w_out[j], rel_bias)
        x = x + conv_ffn(x, f_norm_g[layer], f_w_up[layer], f_conv_w[layer],
                         f_conv_b[layer], f_w_down[layer])
    return rmsnorm(x, final_norm_g)


_drawn_inputs = setup_inputs


def setup_inputs(seed=0):
    import zlib

    import numpy as np

    out = dict(_drawn_inputs(seed))
    spreads = {}
    factors = {'a_hnorm_g': 4.619,
     'kv_norm_g': 8.0,
     'b_norm_g': 8.0,
     'f_norm_g': 2.861,
     'f_conv_b': 5.929,
     'final_norm_g': 2.901}
    for name, (base, spread) in spreads.items():
        noise = np.random.default_rng([zlib.crc32(name.encode()), seed]).standard_normal(out[name].shape)
        drawn = base * np.exp(spread * noise) if base else spread * noise
        out[name] = __import__('jax').numpy.asarray(drawn.astype(out[name].dtype))
    for name, factor in factors.items():
        out[name] = (out[name] * factor).astype(out[name].dtype)
    return out
```

```python
from contextlib import ExitStack

import concourse.bass as bass
import numpy as np
from concourse import mybir

P = 128
D = 1024
S = 256
KD = D // P
NT = S // P
CW = 256
SLOT = KD * CW
RING = 3
AH, DK, DV = 4, 128, 256
FF = 2816
KF = FF // P
PAIRS = FF // CW
NG, BH, DH = 3, 16, 64
HB = CW // DH
NHB = BH // HB
EPS = 1e-6
CAP = 15.0
BUCKETS, MAXD = 32, 2048
GROUPS = ((128, 1), (512, 4), (2048, 16))
DIST = 384
MASKED = -1e30

DOWN_K = ((0, 8), (8, 16), (16, 22))
U_IN, U_AOUT = 0, 12
U_UP0, U_DOWN0 = 16, 38
U_QKV, U_BOUT = 50, 86
U_UP1, U_DOWN1 = 90, 112
U_END = 124
T_IN, T_AOUT = 0, 12
T_UP0, T_DOWN0 = 16, 38
T_QKV, T_BOUT = 42, 78
T_UP1, T_DOWN1 = 82, 104
E_UP0, E_QKV, E_UP1, E_END = 24, 68, 140, 184
FB = (2, 3, 0, 1)
V_A, V_KV, V_B, V_F0, V_F1, V_FIN, V_HN = range(0, 56, 8)

F32 = mybir.dt.float32
F32R = mybir.dt.float32r
ALU = mybir.AluOpType
ACT = mybir.ActivationFunctionType


def distance_tables():
    dist = 255 - np.arange(DIST)
    exact = BUCKETS // 2
    d = np.maximum(dist, 0)
    ratio = np.log(np.maximum(d, 1) / exact) / np.log(MAXD / exact)
    large = np.minimum(exact + (ratio * (BUCKETS - exact)).astype(np.int64), BUCKETS - 1)
    bucket = np.where(d < exact, d, large)
    onehot = (bucket[None, :] == np.arange(BUCKETS)[:, None]).astype(np.float32)
    mask = np.stack([np.where((dist >= 0) & (dist % dil == 0) & (dist <= win), 0.0, MASKED)
                     for win, dil in GROUPS]).astype(np.float32)
    group = np.repeat(np.eye(NG, dtype=np.float32), BH, axis=1)
    return onehot, mask, group


def build(nc, x, a_norm_g, a_w_in, a_b_if, a_hnorm_g, a_w_out, kv_norm_g, w_kv, b_norm_g, b_w_q,
          b_w_out, rel_bias, f_norm_g, f_w_up, f_conv_w, f_conv_b, f_w_down, final_norm_g,
          onehot, mask, group, out):
    ctx = ExitStack()
    with ctx:
        sems = {}

        def sem(name):
            sems[name] = ctx.enter_context(nc.semaphore(name))
            return sems[name]

        at = [(int(nc.sbuf_base) + 63) // 64 * 64]

        def place(name, shape, dt=F32, arena=None):
            cur = at if arena is None else arena
            n = 4
            for s in shape[1:]:
                n *= s
            t = nc.alloc_sbuf_tensor_at(name, shape, dt, offset=cur[0])
            cur[0] += (n + 63) // 64 * 64
            return t

        raw = [place(f"raw{s}", [P, SLOT]) for s in range(RING)]
        whi = [place(f"whi{s}", [P, KD, CW], F32R) for s in range(RING)]
        wlo = [place(f"wlo{s}", [P, KD, CW], F32R) for s in range(RING)]
        X = place("X", [P, KD, S])
        xsA = place("xsA", [P, KD, 2, S], F32R)
        xsB = place("xsB", [P, KD, 2, S], F32R)
        ident = place("ident", [P, P])
        anti = place("anti", [P, P])
        ones = place("ones", [P, P])
        sel = place("sel", [AH, AH, P])
        vrows = place("vrows", [P, 5, P])
        vcols = place("vcols", [P, 5, P])
        acc = place("acc", [P, S])
        sq = place("sq", [P, 2, S])
        root = place("root", [P, S + NT])
        rstd = place("rstd", [P, S + NT])
        bif = place("bif", [AH, 2])
        epsc = place("epsc", [P, 1])
        onec = place("onec", [P, 1])
        bv = place("bv", [NG * BH, DIST])
        oh = place("oh", [BUCKETS, DIST])
        mk = place("mk", [NG, DIST])
        gs = place("gs", [NG, NG * BH])
        rb = place("rb", [BUCKETS, NG * BH])
        base = at[0]

        ar = [base]
        xtm = place("xtm", [P, NT, D], F32, ar)
        XG = place("XG", [P, KD, S], F32, ar)
        wg = place("wg", [P, KD, 2 * AH], F32, ar)
        qT = place("qT", [P, AH, S], F32, ar)
        kT = place("kT", [P, AH, S], F32, ar)
        Vm = place("Vm", [P, NT, AH * DV], F32, ar)
        sig = place("sig", [P, KD, S], F32, ar)
        gz = place("gz", [AH, 2, S], F32, ar)
        gt = place("gt", [AH, 2, S], F32, ar)
        gp = place("gp", [AH, S], F32, ar)
        gl = place("gl", [AH, S], F32, ar)
        gn = place("gn", [AH, S], F32, ar)
        gc = place("gc", [AH, S], F32, ar)
        gm = place("gm", [AH, S], F32, ar)
        gd = place("gd", [AH, S], F32, ar)
        gx = place("gx", [AH, S], F32, ar)
        gones = place("gones", [AH, S], F32, ar)
        cS = place("cS", [P, NT, AH], F32, ar)
        EE = place("EE", [P, AH, 384], F32, ar)
        SD = place("SD", [P, AH, 384], F32, ar)
        EB = place("EB", [P, AH, S], F32, ar)
        den = place("den", [P, AH, S], F32, ar)
        dinv = place("dinv", [P, AH, S], F32, ar)
        assert ar[0] <= nc.sbuf_usable_end, ar[0]
        hm = place("hm", [P, AH, 2, S], F32, [base])
        hsq = place("hsq", [P, AH, 2, S], F32, [base + 8192])
        hroot = place("hroot", [P, AH, S], F32, [base + 2 * 8192 + 256])
        hrs = place("hrs", [P, AH, S], F32, [base + 2 * 8192 + 256 + 4096])

        ar = [base]
        hs = place("hs", [P, KF, 2, S], F32R, ar)
        ub = place("ub", [P, 4, S + 2], F32, ar)
        cb = place("cb", [P, 4, S], F32, ar)
        gb = place("gb", [P, 2, S], F32, ar)
        hb_ = place("hb", [P, 2, S], F32, ar)
        ar = [base]
        QT = place("QT", [P, NG, 2, S], F32, ar)
        KT = place("KT", [P, NG, 2, S], F32, ar)
        Va = place("Va", [P, NT, NG, CW], F32, ar)
        PT = place("PT", [P, HB, 9, P], F32, ar)
        Bi = place("Bi", [P, HB, NG, S], F32, ar)
        SB = place("SB", [P, 2, NG * S], F32, ar)
        ohb = place("ohb", [P, NT, CW], F32, ar)
        aTs = place("aTs", [P, KD, 2, S], F32R, ar)
        nmx = place("nmx", [P, 2 * HB], F32, ar)
        mxx = place("mxx", [P, 2 * HB], F32, ar)
        lsum = place("lsum", [P, 2 * HB], F32, ar)
        linv = place("linv", [P, 2 * HB], F32, ar)
        carry = place("carry", [P, 2], F32, ar)
        assert ar[0] <= nc.sbuf_usable_end, ar[0]
        ar = [base]
        Y = place("Y", [P, KD, S], F32, ar)
        ytm = place("ytm", [P, NT, D], F32, ar)
        assert at[0] <= nc.sbuf_usable_end

        bank = [ctx.enter_context(nc.psum_tensor(f"bank{b}", [P, 512], F32)) for b in range(3)]
        two = [ctx.enter_context(nc.psum_tensor(f"banks{b}", [P, 1024], F32)) for b in (34, 56)]
        bank += [two[0][:, 0:512], two[0][:, 512:1024], two[1][:, 0:512], two[1][:, 512:1024]]
        bank.append(ctx.enter_context(nc.psum_tensor("bank7", [P, 512], F32)))

        bvd = nc.dram_tensor("bias_by_distance", (NG * BH, DIST), F32, kind="Internal")

        raw_in = [sem(f"raw_in{s}") for s in range(RING)]
        hi_done = [sem(f"hi_done{s}") for s in range(RING)]
        lo_done = [sem(f"lo_done{s}") for s in range(RING)]
        w_used = [sem(f"w_used{s}") for s in range(RING)]
        x_in, v_in, c_in, g_in = sem("x_in"), sem("v_in"), sem("c_in"), sem("g_in")
        bv_out, bi_in, y_out = sem("bv_out"), [sem(f"bi_in{h}") for h in range(HB)], sem("y_out")
        consts = sem("consts")
        vt_done = sem("vt_done")
        vcols_done = sem("vcols_done")
        bt_done, bt_copied = sem("bt_done"), sem("bt_copied")
        xt_done = sem("xt_done")
        tile_done = sem("tile_done")
        ev_done = sem("ev_done")
        x_new = sem("x_new")
        sq_done = sem("sq_done")
        acc_zero = sem("acc_zero")
        acc_done = sem("acc_done")
        xhi_done = sem("xhi_done")
        xlo_done = sem("xlo_done")
        xg_done = sem("xg_done")
        ss_done = sem("ss_done")
        root_done, rstd_done = sem("root_done"), sem("rstd_done")
        gates_ps, gseq, gact = sem("gates_ps"), sem("gseq"), sem("gact")
        gates_done, gnorm_done = sem("gates_done"), sem("gnorm_done")
        ct_done, mb_done, eb_done = sem("ct_done"), sem("mb_done"), sem("eb_done")
        cs_done, eb_copied = sem("cs_done"), sem("eb_copied")
        ee_done, dm_exp, dm_done = sem("ee_done"), sem("dm_exp"), sem("dm_done")
        s_done, sd_done = sem("s_done"), sem("sd_done")
        den_done, den_abs, dmax_done, dinv_done = (sem("den_done"), sem("den_abs"),
                                                   sem("dmax_done"), sem("dinv_done"))
        num_done, hm_done, hsq_done = sem("num_done"), sem("hm_done"), sem("hsq_done")
        hss_done, hroot_done, hrs_done = sem("hss_done"), sem("hroot_done"), sem("hrs_done")
        sig_done, hn_done, hg_done = sem("sig_done"), sem("hn_done"), sem("hg_done")
        mhi_done, mlo_done = sem("mhi_done"), sem("mlo_done")
        pad_done = sem("pad_done")
        t1_done, cA_done, cB_done = sem("t1_done"), sem("cA_done"), sem("cB_done")
        silu_done, mul_done = sem("silu_done"), sem("mul_done")
        hhi_done, hlo_done = sem("hhi_done"), sem("hlo_done")
        sc_done, smax_done, nmx_done = sem("sc_done"), sem("smax_done"), sem("nmx_done")
        exp_done, tr_done, pt_done = sem("exp_done"), sem("tr_done"), sem("pt_done")
        pv_done, linv_done, o_done = sem("pv_done"), sem("linv_done"), sem("o_done")
        flip_done, ahi_done, alo_done = sem("flip_done"), sem("ahi_done"), sem("alo_done")
        yn_done, yt_done, ytm_done = sem("yn_done"), sem("yt_done"), sem("ytm_done")

        block = ctx.enter_context(nc.Block())

        def rnd(n, i=0, step=0):
            return n // RING + i * (step // RING) if step else n // RING

        def ge(eng, s, v):
            if not (isinstance(v, int) and v <= 0):
                eng.wait_ge(s, v)

        def col(tile, c):
            return vcols[:, tile, c:c + 1]

        @block.sync
        def _(sp):
            def load(n, i, step, src, nk):
                s = n % RING
                if n >= RING:
                    sp.wait_ge(lo_done[s], rnd(n, i, step))
                sp.dma_start(raw[s][:, 0:nk * CW].rearrange("p (k c) -> p k c", c=CW),
                             src).then_inc(raw_in[s], 16)

            def cols(w, c):
                return w.rearrange("(k p) n -> p k n", p=P)[:, :, bass.ds(c, CW)]

            sp.dma_start(xtm[:, :, :], x[0].rearrange("(t p) d -> p t d", p=P)).then_inc(x_in, 16)
            w_in = a_w_in[0]
            for u in range(12):
                load(U_IN + u, 0, 0, cols(w_in, u * CW), KD)
            for u in range(4):
                load(U_AOUT + u, 0, 0, cols(a_w_out[0], u * CW), KD)

            def ffn(layer, u_up, u_down):
                w = f_w_up[layer]

                def pair(n, i, step, p):
                    load(n, i, step, cols(w, p * CW), KD)
                    load(n + 1, i, step, cols(w, p * CW + FF), KD)

                pair(u_up, 0, 0, 0)
                with sp.Fori(0, 3) as i:
                    for j in range(3):
                        pair(u_up + 2 + 2 * j, i, 6, i * 3 + (1 + j))
                pair(u_up + 20, 0, 0, PAIRS - 1)
                wd = f_w_down[layer].rearrange("(k p) n -> p k n", p=P)
                with sp.Fori(0, 4) as i:
                    for j, (k0, k1) in enumerate(DOWN_K):
                        load(u_down + j, i, 3, wd[:, k0:k1, bass.ds(i * CW, CW)], k1 - k0)

            ffn(0, U_UP0, U_DOWN0)
            with sp.Fori(0, NHB) as i:
                for g in range(NG):
                    load(U_QKV + 2 * g, i, 9, cols(b_w_q[0], i * CW + g * D), KD)
                    load(U_QKV + 2 * g + 1, i, 9, cols(w_kv, i * CW + g * D), KD)
                for g in range(NG):
                    load(U_QKV + 6 + g, i, 9, cols(w_kv, i * CW + (NG + g) * D), KD)
            for u in range(4):
                load(U_BOUT + u, 0, 0, cols(b_w_out[0], u * CW), KD)
            ffn(1, U_UP1, U_DOWN1)
            for t in range(NT):
                sp.wait_ge(ytm_done, 4 * (t + 1))
                sp.dma_start(out[0, t * P:(t + 1) * P, :], ytm[:, t, :]).then_inc(y_out, 16)
            sp.wait_ge(y_out, 16 * NT)
            sp.wait_ge(bv_out, 16)

        @block.gpsimd
        def _(pool):
            g = nc.gpsimd
            g.memset(ident[:], 0.0).then_inc(consts, 1)
            g.memset(anti[:], 0.0).then_inc(consts, 1)
            g.memset(sel[:], 0.0).then_inc(consts, 1)
            g.memset(ones[:], 1.0).then_inc(consts, 1)
            g.memset(epsc[:], EPS).then_inc(consts, 1)
            g.memset(onec[:], 1.0).then_inc(consts, 1)
            g.memset(gones[:], 1.0).then_inc(consts, 1)
            pool.wait_ge(consts, 7)
            g.affine_select(out=ident[:], in_=ident[:], compare_op=ALU.not_equal, fill=1.0, base=0,
                            pattern=[[-1, P]], channel_multiplier=1).then_inc(consts, 1)
            g.affine_select(out=anti[:], in_=anti[:], compare_op=ALU.not_equal, fill=1.0,
                            base=-(P - 1), pattern=[[1, P]], channel_multiplier=1).then_inc(consts, 1)
            g.affine_select(out=sel[:], in_=sel[:], compare_op=ALU.not_equal, fill=1.0, base=0,
                            pattern=[[-1, AH], [0, P]], channel_multiplier=1).then_inc(consts, 1)

            def lo(n, i=0, step=0):
                s = n % RING
                pool.wait_ge(hi_done[s], rnd(n, i, step) + 1)
                g.tensor_tensor(wlo[s][:, :, :], raw[s][:, :].rearrange("p (k c) -> p k c", c=CW),
                                whi[s][:, :, :].bitcast(F32), ALU.subtract).then_inc(lo_done[s], 1)

            for n in range(U_IN, 9):
                if n % RING:
                    lo(n)
            pool.wait_ge(dm_exp, 2 * AH)
            g.affine_select(out=EE[:, :, 0:S], in_=EE[:, :, 0:S], compare_op=ALU.is_ge, fill=0.0,
                            base=0, pattern=[[0, AH], [1, S]], channel_multiplier=-1)\
                .then_inc(dm_done, 1)
            g.affine_select(out=EE[:, :, S:384], in_=EE[:, :, S:384], compare_op=ALU.is_ge,
                            fill=0.0, base=0, pattern=[[0, AH], [1, P]], channel_multiplier=-1)\
                .then_inc(dm_done, 1)
            with pool.Fori(0, (U_END - 10) // RING) as i:
                for n in (10, 11):
                    lo(n, i, RING)

        @block.scalar
        def _(act):
            a = nc.scalar

            def hi(n, i=0, step=0):
                s = n % RING
                act.wait_ge(raw_in[s], (rnd(n, i, step) + 1) * 16)
                if n >= RING:
                    act.wait_ge(w_used[s], rnd(n, i, step))
                a.activation(whi[s][:, :, :], raw[s][:, :].rearrange("p (k c) -> p k c", c=CW),
                             ACT.Copy).then_inc(hi_done[s], 1)

            def post(k, q, sets, i=0, dq=0):
                act.wait_ge(x_new, q + i * dq + 1)
                if q >= 2:
                    act.wait_ge(acc_done, q + i * dq - 1)
                a.activation(sq[:, q % 2, :], X[:, bass.ds(k, 1), :].rearrange("p a t -> p (a t)"),
                             ACT.Square).then_inc(sq_done, 1)
                for dst, gain in sets:
                    a.activation(dst[:, bass.ds(k, 1), 0, :], X[:, bass.ds(k, 1), :], ACT.Copy,
                                 scale=vcols[:, 0, bass.ds(k + gain, 1)]).then_inc(xhi_done, 1)

            def root_of(s, width, b):
                act.wait_ge(ss_done, s + 1)
                if s:
                    act.wait_ge(rstd_done, s)
                a.activation(root[:, 0:width], bank[b][:, 0:width], ACT.Sqrt, bias=epsc[:, 0:1],
                             scale=1.0 / D).then_inc(root_done, 1)

            for r, v in ((V_A, a_norm_g), (V_KV, kv_norm_g), (V_B, b_norm_g), (V_FIN, final_norm_g),
                         (V_HN, a_hnorm_g)):
                flat = v if len(v.shape) == 1 else v.rearrange("a n -> (a n)") if len(v.shape) == 2 \
                    else v.rearrange("a h n -> (a h n)")
                act.dma_start(vrows[r:r + 8, 0, :], flat.rearrange("(k p) -> k p", p=P))\
                    .then_inc(v_in, 16)
            act.dma_start(vrows[V_F0:V_F0 + 16, 0, :], f_norm_g.rearrange("l (k p) -> (l k) p", p=P))\
                .then_inc(v_in, 16)
            for layer in range(2):
                act.dma_start(vrows[0:88, 1 + 2 * layer, :],
                              f_conv_w[layer, 0:2].rearrange("j (t p) -> (j t) p", p=P))\
                    .then_inc(v_in, 16)
                act.dma_start(vrows[0:44, 2 + 2 * layer, :],
                              f_conv_w[layer, 2].rearrange("(t p) -> t p", p=P)).then_inc(v_in, 16)
                act.dma_start(vrows[44:88, 2 + 2 * layer, :],
                              f_conv_b[layer].rearrange("(t p) -> t p", p=P)).then_inc(v_in, 16)
            act.dma_start(wg[:, :, :], a_w_in[0].rearrange("(k p) n -> p k n", p=P)
                          [:, :, 3072:3080]).then_inc(g_in, 16)
            with nc.allow_non_contiguous_dma(reason="8 numbers"):
                act.dma_start(bif[:, :], a_b_if[0].rearrange("(j p) -> p j", p=AH)).then_inc(g_in, 16)
            act.dma_start(oh[:], onehot).then_inc(c_in, 16)
            act.dma_start(mk[:], mask).then_inc(c_in, 16)
            act.dma_start(gs[:], group).then_inc(c_in, 16)
            act.dma_start(rb[:], rel_bias).then_inc(c_in, 16)

            hi(0)
            act.wait_ge(vcols_done, 5)
            for k in range(KD):
                post(k, k, ((xsA, V_A),))
            hi(1)
            root_of(0, S + NT, 7)
            hi(2)
            act.wait_ge(bt_copied, 1)
            act.dma_start(bvd.ap(), bv[:, :]).then_inc(bv_out, 16)
            for u in range(12):
                if u == 4:
                    act.wait_ge(gseq, 2)
                    a.activation(gt[:, :, :], gz[:, :, :], ACT.Tanh, scale=1.0 / CAP).then_inc(gact, 1)
                    act.wait_ge(gact, 1)
                    a.activation(gp[:, :], gt[:, 1, :], ACT.Exp,
                                 scale=-CAP).then_inc(gact, 1)
                    act.wait_ge(gact, 2)
                    a.activation(gl[:, :], gp[:, :], ACT.Ln, bias=onec[0:AH, 0:1])\
                        .then_inc(gact, 1)
                    act.wait_ge(gseq, 6)
                    a.activation(gx[:, :], gd[:, :], ACT.Exp).then_inc(gates_done, 1)
                if u == 7:
                    for b in range(2):
                        act.wait_ge(eb_done, b + 1)
                        a.activation(EB[:, 2 * b:2 * b + 2, :],
                                     bank[(3, 7)[b]][:, :].rearrange("p (h t) -> p h t", h=2),
                                     ACT.Copy).then_inc(eb_copied, 1)
                    for e in range(2 * AH):
                        h, st = divmod(e, 2)
                        c = slice(0, S) if st == 0 else slice(S, 384)
                        act.wait_ge(ee_done, e + 1)
                        a.activation(EE[:, h, c], EE[:, h, c], ACT.Exp, scale=-1.0)\
                            .then_inc(dm_exp, 1)
                if u in (9, 10):
                    for h in (0, 1) if u == 9 else (2, 3):
                        act.wait_ge(den_done, h + 1)
                        a.activation(den[:, h, :], bank[7][:, 0:S], ACT.Abs).then_inc(den_abs, 1)
                        act.wait_ge(hm_done, h + 1)
                        a.activation(hsq[:, h, :, :], hm[:, h, :, :], ACT.Square)\
                            .then_inc(hsq_done, 1)
                if u == 11:
                    for b in range(2):
                        act.wait_ge(hss_done, b + 1)
                        a.activation(hroot[:, 2 * b:2 * b + 2, :],
                                     bank[3 + b][:, :].rearrange("p (h t) -> p h t", h=2),
                                     ACT.Sqrt, bias=epsc[:, 0:1], scale=1.0 / DV)\
                            .then_inc(hroot_done, 1)
                hi(u + 3)
            for k in range(KD):
                act.wait_ge(ev_done, 16 + k + 1)
                a.activation(sig[:, k, :], sig[:, k, :], ACT.Sigmoid).then_inc(sig_done, 1)
            for k in range(KD):
                act.wait_ge(hg_done, k + 1)
                a.activation(xsB[:, k, 0, :], hm[:, k // 2, k % 2, :], ACT.Copy)\
                    .then_inc(mhi_done, 1)
            for u in range(4):
                for c in range(2):
                    k = 2 * u + c
                    post(k, 8 + k, ((xsA, V_F0),))
                hi(U_AOUT + u + 3)

            def ffn(layer, u_up, e_up, u_down, q0, sets, s):
                f0, p0 = 4 * PAIRS * layer, PAIRS * layer
                vB = 2 + 2 * layer

                def first_tap(p, g):
                    for c in range(2):
                        j = 2 * g + c
                        act.wait_ge(ev_done, 4 * p + (e_up + j + 1))
                        ge(act, mul_done if g else silu_done, p + p0)
                        ch = p * 2 + (KF * g + c)
                        a.activation(cb[:, j, :], ub[:, j, 2:S + 2], ACT.Identity,
                                     scale=vcols[:, vB, bass.ds(ch, 1)],
                                     bias=vcols[:, vB, bass.ds(ch + 2 * KF, 1)])\
                            .then_inc(t1_done, 1)

                def h_hi(p):
                    act.wait_ge(mul_done, p + (p0 + 1))
                    a.activation(hs[:, bass.ds(p * 2, 2), 0, :], hb_[:, :, :], ACT.Copy)\
                        .then_inc(hhi_done, 1)

                def pair(n, p, i, step, first):
                    first_tap(p, 0)
                    if not first:
                        h_hi(p - 1)
                    hi(n + 3, i, step)
                    first_tap(p, 1)
                    act.wait_ge(cB_done, 4 * p + (f0 + 2))
                    ge(act, mul_done, p + p0)
                    a.activation(gb[:, :, :], cb[:, 0:2, :], ACT.Silu).then_inc(silu_done, 1)
                    hi(n + 4, i, step)

                root_of(s, S, 6)
                pair(u_up, 0, 0, 0, True)
                with act.Fori(0, 3) as i:
                    for j in range(3):
                        pair(u_up + 2 + 2 * j, i * 3 + (1 + j), i, 6, False)
                pair(u_up + 20, PAIRS - 1, 0, 0, False)
                h_hi(PAIRS - 1)
                with act.Fori(0, 3) as i:
                    hi(u_down + 3, i, 3)
                    hi(u_down + 4, i, 3)
                    for c in range(2):
                        post(i * 2 + c, q0 + c, sets, i, 2)
                    hi(u_down + 5, i, 3)
                for n in (12, 13):
                    if u_down + n < U_END:
                        hi(u_down + n)
                for k in (6, 7):
                    post(k, q0 + k, sets)
                if u_down + 14 < U_END:
                    hi(u_down + 14)

            ffn(0, U_UP0, E_UP0, U_DOWN0, 16, ((xsA, V_KV), (xsB, V_B)), 1)

            root_of(2, S + NT, 7)
            with act.Fori(0, NHB) as i:
                for h in range(HB):
                    if h == 0:
                        act.wait_ge(bv_out, 16)
                    src = bass.AP(bvd, (i * HB + h) * DIST, [[1, P], [BH * DIST, NG], [1, S]])
                    act.dma_start(Bi[:, h, :, :], src).then_inc(bi_in[h], 16)

                def soft(s):
                    h, tt = divmod(s, 2)
                    w = NG * P * (1 + tt)
                    act.wait_ge(nmx_done, i * 8 + (s + 1))
                    a.activation(SB[:, s % 2, 0:w], SB[:, s % 2, 0:w], ACT.Exp,
                                 bias=nmx[:, s:s + 1], accum_out=lsum[:, s:s + 1])\
                        .then_inc(exp_done, 1)

                for u in range(6):
                    hi(U_QKV + u + 3, i, 9)
                for u in range(6, 9):
                    soft(2 * (u - 6))
                    soft(2 * (u - 6) + 1)
                    hi(U_QKV + u + 3, i, 9)
                soft(6)
                soft(7)
                for c in range(2):
                    act.wait_ge(flip_done, i * 2 + (c + 1))
                    a.activation(aTs[:, bass.ds(i * 2 + c, 1), 0, :], bank[7][:, S:2 * S]
                                 .rearrange("p (a t) -> p a t", a=1), ACT.Copy)\
                        .then_inc(ahi_done, 1)
            for u in range(4):
                for c in range(2):
                    k = 2 * u + c
                    post(k, 24 + k, ((xsB, V_F1),))
                hi(U_BOUT + u + 3)
            ffn(1, U_UP1, E_UP1, U_DOWN1, 32, (), 3)
            root_of(4, S, 6)

        @block.vector
        def _(dve):
            v = nc.vector

            def lo(n, i=0, step=0):
                if n % RING or n >= U_END:
                    return
                dve.wait_ge(hi_done[0], rnd(n, i, step) + 1)
                v.tensor_tensor(wlo[0][:, :, :], raw[0][:, :].rearrange("p (k c) -> p k c", c=CW),
                                whi[0][:, :, :].bitcast(F32), ALU.subtract).then_inc(lo_done[0], 1)

            def acc_clear(q):
                if q:
                    dve.wait_ge(ss_done, q // 8)
                v.memset(acc[:, :], 0.0).then_inc(acc_zero, 1)
                dve.wait_ge(acc_zero, q // 8 + 1)

            def post(k, q, x0, sets, i=0, dq=0):
                for m, (dst, gain) in enumerate(sets):
                    dve.wait_ge(xhi_done, x0 + m + 1 + i * (dq * len(sets)))
                    v.scalar_tensor_tensor(dst[:, bass.ds(k, 1), 1, :], X[:, bass.ds(k, 1), :],
                                           vcols[:, 0, bass.ds(k + gain, 1)],
                                           dst[:, bass.ds(k, 1), 0, :].bitcast(F32),
                                           ALU.mult, ALU.subtract).then_inc(xlo_done, 1)
                dve.wait_ge(sq_done, q + i * dq + 1)
                ge(dve, acc_done, q + i * dq)
                v.tensor_tensor(acc[:, :], acc[:, :], sq[:, q % 2, :], ALU.add)\
                    .then_inc(acc_done, 1)

            def rstd_of(s, width):
                dve.wait_ge(root_done, s + 1)
                v.reciprocal(rstd[:, 0:width], root[:, 0:width]).then_inc(rstd_done, 1)
                dve.wait_ge(rstd_done, s + 1)

            def complete(c, m, n, i=0, step=0):
                if c:
                    dve.wait_ge(w_used[n % RING], rnd(n, i, step) + 1)
                else:
                    dve.wait_ge(tile_done, m + 1)

            def residual(k, c, m, n, b, i=0, step=0):
                complete(c, m, n, i, step)
                xk = X[:, bass.ds(k, 1), :].rearrange("p a t -> p (a t)")
                v.tensor_tensor(xk, xk, bank[b][:, 0:S], ALU.add).then_inc(x_new, 1)

            for n in range(5):
                dve.wait_ge(vt_done, max(n + 1, 4))
                w = 56 if n == 0 else 88
                src = bank[7][:, n * P:n * P + w] if n < 4 else bank[2][:, 0:w]
                v.tensor_copy(vcols[:, n, 0:w], src).then_inc(vcols_done, 1)
            acc_clear(0)
            for q in range(4):
                dve.wait_ge(xt_done, q + 1)
                for c in range(2):
                    v.tensor_copy(X[:, 2 * q + c, :], bank[3 + q][:, c * S:(c + 1) * S])\
                        .then_inc(x_new, 1)
            dve.wait_ge(bt_done, 1)
            v.tensor_copy(bv[:, :], bank[1][0:NG * BH, 0:DIST]).then_inc(bt_copied, 1)
            dve.wait_ge(vcols_done, 5)
            lo(0)
            for k in range(KD):
                dve.wait_ge(x_new, k + 1)
                post(k, k, k, ((xsA, V_A),))
                v.tensor_scalar(XG[:, k, :], X[:, k, :], col(0, V_A + k), None, ALU.mult)\
                    .then_inc(xg_done, 1)
            rstd_of(0, S + NT)
            for u in range(12):
                lo(u + 2)
                if u == 4:
                    for j in range(2):
                        dve.wait_ge(gates_ps, 1)
                        v.tensor_tensor(gt[:, j, :], bank[3][0:AH, j * S:(j + 1) * S],
                                        rstd[0:AH, 0:S], ALU.mult).then_inc(gnorm_done, 1)
                    for j in range(2):
                        dve.wait_ge(gnorm_done, j + 1)
                        v.tensor_scalar(gz[:, j, :], gt[:, j, :], bif[:, j:j + 1], None, ALU.add)\
                            .then_inc(gseq, 1)
                    dve.wait_ge(gact, 3)
                    v.tensor_tensor_scan(gn[:, :], gones[:, :], gl[:, :], 0.0, ALU.mult, ALU.add)\
                        .then_inc(gseq, 1)
                    dve.wait_ge(gseq, 3)
                    v.scalar_tensor_tensor(gc[:, :], gt[:, 0, :], CAP, gn[:, :], ALU.mult, ALU.add)\
                        .then_inc(gseq, 1)
                    dve.wait_ge(gseq, 4)
                    v.tensor_tensor_scan(gm[:, :], gc[:, :], gc[:, :], 0.0, ALU.max, ALU.max)\
                        .then_inc(gseq, 1)
                    dve.wait_ge(gseq, 5)
                    v.tensor_tensor(gd[:, :], gn[:, :], gm[:, :], ALU.subtract).then_inc(gseq, 1)
                if u == 7:
                    dve.wait_ge(ct_done, 1)
                    v.tensor_copy(cS[:, :, :].rearrange("p s h -> p (s h)"),
                                  bank[4][:, 0:NT * AH]).then_inc(cs_done, 1)
                    dve.wait_ge(cs_done, 1)
                    for h in range(AH):
                        dve.wait_ge(mb_done, 2 * (h // 2) + 2)
                        m = bank[5 + h // 2][:, (h % 2) * S:(h % 2 + 1) * S]
                        v.tensor_scalar(EE[:, h, 0:S], m, cS[:, 0, h:h + 1], 0.0,
                                        ALU.subtract, ALU.max).then_inc(ee_done, 1)
                        v.tensor_scalar(EE[:, h, S:384], m[:, P:S], cS[:, 1, h:h + 1], 0.0,
                                        ALU.subtract, ALU.max).then_inc(ee_done, 1)
                if u == 8:
                    for h in range(AH):
                        dve.wait_ge(s_done, h + 1)
                        dve.wait_ge(dm_done, 2)
                        v.scalar_tensor_tensor(SD[:, h, :], bank[3 + h][:, 0:384], DK ** -0.5,
                                               EE[:, h, :], ALU.mult, ALU.mult)\
                            .then_inc(sd_done, 1)
                if u in (9, 10):
                    for h in (0, 1) if u == 9 else (2, 3):
                        dve.wait_ge(den_abs, h + 1)
                        v.tensor_tensor(den[:, h, :], den[:, h, :], EB[:, h, :], ALU.max)\
                            .then_inc(dmax_done, 1)
                        dve.wait_ge(dmax_done, h + 1)
                        v.reciprocal(dinv[:, h, :], den[:, h, :]).then_inc(dinv_done, 1)
                        dve.wait_ge(dinv_done, h + 1)
                        dve.wait_ge(num_done, h + 1)
                        v.tensor_tensor(hm[:, h, :, :],
                                        bank[3 + h][:, :].rearrange("p (c t) -> p c t", c=2),
                                        dinv[:, h:h + 1, :].to_broadcast([P, 2, S]), ALU.mult)\
                            .then_inc(hm_done, 1)
                if u == 11:
                    for b in range(2):
                        dve.wait_ge(hroot_done, b + 1)
                        v.reciprocal(hrs[:, 2 * b:2 * b + 2, :], hroot[:, 2 * b:2 * b + 2, :])\
                            .then_inc(hrs_done, 1)
                    for h in range(AH):
                        dve.wait_ge(hrs_done, h // 2 + 1)
                        v.tensor_tensor(hm[:, h, :, :], hm[:, h, :, :],
                                        hrs[:, h:h + 1, :].to_broadcast([P, 2, S]), ALU.mult)\
                            .then_inc(hn_done, 1)
                for c in range(2):
                    t = 2 * u + c
                    complete(c, T_IN + u, U_IN + u)
                    ps = bank[t % 3][:, 0:S]
                    if u < 2:
                        o = v.tensor_tensor(qT[:, 2 * u + c, :], ps, rstd[:, 0:S], ALU.mult)
                    elif u < 4:
                        o = v.tensor_tensor(kT[:, 2 * (u - 2) + c, :], ps, rstd[:, 0:S], ALU.mult)
                    elif u < 8:
                        o = v.tensor_scalar(Vm[:, c, (u - 4) * CW:(u - 3) * CW], ps,
                                            rstd[:, S + c:S + c + 1], None, ALU.mult)
                    else:
                        o = v.tensor_tensor(sig[:, 2 * (u - 8) + c, :], ps, rstd[:, 0:S], ALU.mult)
                    o.then_inc(ev_done, 1)

            def m_lo(k):
                dve.wait_ge(mhi_done, k + 1)
                v.tensor_tensor(xsB[:, k, 1, :], hm[:, k // 2, k % 2, :],
                                xsB[:, k, 0, :].bitcast(F32), ALU.subtract).then_inc(mlo_done, 1)

            for k in range(KD):
                dve.wait_ge(sig_done, k + 1)
                dve.wait_ge(hn_done, k // 2 + 1)
                hk = hm[:, k // 2, k % 2, :]
                v.scalar_tensor_tensor(hk, hk, col(0, V_HN + k), sig[:, k, :], ALU.mult, ALU.mult)\
                    .then_inc(hg_done, 1)
                if k:
                    m_lo(k - 1)
            m_lo(KD - 1)

            def outproj(u0, t0, q0, x0, sets):
                acc_clear(q0)
                for u in range(4):
                    lo(u0 + u + 2)
                    for c in range(2):
                        residual(2 * u + c, c, t0 + u, u0 + u, c)
                    for c in range(2):
                        dve.wait_ge(x_new, q0 + 2 * u + c + 1)
                        post(2 * u + c, q0 + 2 * u + c, x0 + 2 * u + c, sets)

            outproj(U_AOUT, T_AOUT, 8, 8, ((xsA, V_F0),))

            def ffn(layer, u_up, t_up, u_down, t_down, q0, x0, sets, s):
                f0, p0 = 4 * PAIRS * layer, PAIRS * layer
                vA = 1 + 2 * layer

                def read_out(p, g, n, i, step):
                    for c in range(2):
                        j = 2 * g + c
                        complete(c, p * 2 + (t_up + g), n + g, i, step)
                        ge(dve, cB_done, 4 * p + (f0 - 4 + j + 1))
                        v.tensor_tensor(ub[:, j, 2:S + 2], bank[FB[j]][:, 0:S], rstd[:, 0:S], ALU.mult)\
                            .then_inc(ev_done, 1)

                def taps(p, g):
                    for c in range(2):
                        j = 2 * g + c
                        dve.wait_ge(t1_done, 4 * p + (f0 + j + 1))
                        v.scalar_tensor_tensor(cb[:, j, :], ub[:, j, 1:S + 1],
                                               vcols[:, vA, bass.ds(p * 2 + (KF * g + c + 44), 1)],
                                               cb[:, j, :], ALU.mult, ALU.add).then_inc(cA_done, 1)
                    for c in range(2):
                        j = 2 * g + c
                        dve.wait_ge(cA_done, 4 * p + (f0 + j + 1))
                        v.scalar_tensor_tensor(cb[:, j, :], ub[:, j, 0:S],
                                               vcols[:, vA, bass.ds(p * 2 + (KF * g + c), 1)],
                                               cb[:, j, :], ALU.mult, ALU.add).then_inc(cB_done, 1)

                def product(p):
                    dve.wait_ge(silu_done, p + (p0 + 1))
                    dve.wait_ge(cB_done, 4 * p + (f0 + 4))
                    v.tensor_tensor(hb_[:, :, :], gb[:, :, :], cb[:, 2:4, :], ALU.mult)\
                        .then_inc(mul_done, 1)

                def h_lo(p):
                    dve.wait_ge(hhi_done, p + (p0 + 1))
                    v.tensor_tensor(hs[:, bass.ds(2 * p, 2), 1, :], hb_[:, :, :],
                                    hs[:, bass.ds(2 * p, 2), 0, :].bitcast(F32), ALU.subtract)\
                        .then_inc(hlo_done, 1)

                def pair(n, p, i, step, first):
                    lo(n + 2, i, step)
                    read_out(p, 0, n, i, step)
                    if not first:
                        taps(p - 1, 1)
                        product(p - 1)
                    lo(n + 3, i, step)
                    read_out(p, 1, n, i, step)
                    taps(p, 0)
                    if not first:
                        h_lo(p - 1)

                v.memset(ub[:, :, 0:2], 0.0).then_inc(pad_done, 1)
                dve.wait_ge(pad_done, layer + 1)
                rstd_of(s, S)
                pair(u_up, 0, 0, 0, True)
                with dve.Fori(0, 3) as i:
                    for j in range(3):
                        pair(u_up + 2 + 2 * j, i * 3 + (1 + j), i, 6, False)
                pair(u_up + 20, PAIRS - 1, 0, 0, False)
                taps(PAIRS - 1, 1)
                product(PAIRS - 1)
                h_lo(PAIRS - 1)
                acc_clear(q0)

                def column(i, n, ii, step, last):
                    lo(n + 2, ii, step)
                    lo(n + 3, ii, step)
                    lo(n + 4, ii, step)
                    m = 6 if last else 0
                    for c in range(2):
                        residual(i * 2 + c, c, i + t_down, n + 2, 4 + c, ii, step)
                    for c in range(2):
                        dve.wait_ge(x_new, q0 + m + c + 1 + ii * (0 if last else 2))
                        post(i * 2 + c, q0 + m + c, x0 + (m + c) * len(sets), sets, ii,
                             0 if last else 2)

                with dve.Fori(0, 3) as i:
                    column(i, u_down, i, 3, False)
                column(3, u_down + 9, 0, 0, True)

            ffn(0, U_UP0, T_UP0, U_DOWN0, T_DOWN0, 16, 16, ((xsA, V_KV), (xsB, V_B)), 1)

            rstd_of(2, S + NT)
            with dve.Fori(0, NHB) as i:
                def evac(u, c):
                    t = 2 * u + c
                    complete(c, i * 9 + (T_QKV + u), U_QKV + u, i, 9)
                    ps = bank[t % 3][:, 0:S]
                    g, is_k = divmod(u, 2)
                    if u < 6 and not is_k:
                        o = v.scalar_tensor_tensor(
                            QT[:, g, c, :].rearrange("p (a t) -> p a t", a=NT)[:, :, ::-1],
                            ps.rearrange("p (a t) -> p a t", a=NT), DH ** -0.5,
                            rstd[:, 0:S].rearrange("p (a t) -> p a t", a=NT), ALU.mult, ALU.mult)
                    elif u < 6:
                        o = v.tensor_tensor(KT[:, g, c, :], ps, rstd[:, 0:S], ALU.mult)
                    else:
                        o = v.tensor_scalar(Va[:, c, u - 6, :], ps, rstd[:, S + c:S + c + 1], None,
                                            ALU.mult)
                    o.then_inc(ev_done, 1)

                def biased(s):
                    h, tt = divmod(s, 2)
                    w = P * (1 + tt)
                    dve.wait_ge(sc_done, i * 8 + (s + 1))
                    if tt == 0:
                        dve.wait_ge(bi_in[h], i * 16 + 16)
                    if s >= 2:
                        dve.wait_ge(tr_done, i * 8 + (s - 1))
                    v.memset(carry[:, s % 2:s % 2 + 1], 0.0)
                    bb = Bi[:, h, :, :] if tt else Bi[:, h, :, P:S]
                    v.tensor_tensor_reduce(
                        out=SB[:, s % 2, 0:NG * w].rearrange("p (g f) -> p g f", g=NG),
                        in0=two[0][:, 0:NG * w].rearrange("p (g f) -> p g f", g=NG), in1=bb,
                        scale=1.0, scalar=-3e38, op0=ALU.add, op1=ALU.max,
                        accum_out=mxx[:, s:s + 1]).then_inc(smax_done, 1)
                    dve.wait_ge(smax_done, i * 8 + (s + 1))
                    v.tensor_scalar(nmx[:, s:s + 1], mxx[:, s:s + 1], -1.0, None, ALU.mult)\
                        .then_inc(nmx_done, 1)

                def pt_copy(s):
                    h, tt = divmod(s, 2)
                    w = NG * (1 + tt)
                    dve.wait_ge(tr_done, i * 8 + (s + 1))
                    v.tensor_copy(PT[:, h, 3 * tt:3 * tt + w, :].rearrange("p b q -> p (b q)"),
                                  two[1][:, 0:w * P]).then_inc(pt_done, 1)

                def normed(h):
                    dve.wait_ge(exp_done, i * 8 + 2 * h + 2)
                    v.reciprocal(linv[:, 2 * h:2 * h + 2], lsum[:, 2 * h:2 * h + 2])\
                        .then_inc(linv_done, 1)
                    dve.wait_ge(linv_done, i * HB + (h + 1))
                    dve.wait_ge(pv_done, i * HB + (h + 1))
                    for tt in range(NT):
                        v.tensor_scalar(ohb[:, tt, h * DH:(h + 1) * DH],
                                        bank[7][:, tt * DH:(tt + 1) * DH],
                                        linv[:, 2 * h + tt:2 * h + tt + 1], None, ALU.mult)\
                            .then_inc(o_done, 1)

                def a_lo(c):
                    dve.wait_ge(ahi_done, i * 2 + (c + 1))
                    v.tensor_tensor(aTs[:, bass.ds(i * 2 + c, 1), 1, :],
                                    bank[7][:, S:2 * S].rearrange("p (a t) -> p a t", a=1),
                                    aTs[:, bass.ds(i * 2 + c, 1), 0, :].bitcast(F32), ALU.subtract)\
                        .then_inc(alo_done, 1)

                for u in range(6):
                    lo(U_QKV + u + 2, i, 9)
                    evac(u, 0)
                    evac(u, 1)
                biased(0)
                for m in range(6):
                    if m % 2 == 0:
                        lo(U_QKV + 6 + m // 2 + 2, i, 9)
                    evac(6 + m // 2, m % 2)
                    pt_copy(m)
                    biased(m + 1)
                normed(0)
                pt_copy(6)
                biased(7)
                normed(1)
                a_lo(0)
                normed(2)
                pt_copy(7)
                normed(3)
                a_lo(1)
            outproj(U_BOUT, T_BOUT, 24, 32, ((xsB, V_F1),))
            ffn(1, U_UP1, T_UP1, U_DOWN1, T_DOWN1, 32, 40, (), 3)

            rstd_of(4, S)
            for k in range(KD):
                v.scalar_tensor_tensor(Y[:, k, :], X[:, k, :], col(0, V_FIN + k), rstd[:, 0:S],
                                       ALU.mult, ALU.mult).then_inc(yn_done, 1)
            for m in range(8):
                tt, q = divmod(m, 4)
                dve.wait_ge(yt_done, m + 1)
                v.tensor_copy(ytm[:, tt, q * CW:(q + 1) * CW], bank[m % 4][:, 0:CW])\
                    .then_inc(ytm_done, 1)

        @block.tensor
        def _(pe):
            t_ = nc.tensor

            def three(ps, hi_w, lo_w, hi_x, lo_x, first, last):
                t_.matmul(ps, hi_w, hi_x, start=first, stop=False)
                t_.matmul(ps, hi_w, lo_x, start=False, stop=False)
                return t_.matmul(ps, lo_w, hi_x, start=False, stop=last)

            def unit(n, xs, banks, i=0, step=0, ks=(0, KD), ktot=KD, wait_bank=(), k_wait=None,
                     token_major=False):
                s = n % RING
                pe.wait_ge(lo_done[s], rnd(n, i, step) + 1)
                k0, k1 = ks
                order = [(k, c) for k in range(k0, k1) for c in range(2)] if k_wait else \
                    [(k, c) for c in range(2) for k in range(k0, k1)]
                for k, c in order:
                    if k_wait and c == 0:
                        k_wait(k)
                    if k == k0 and c < len(wait_bank) and wait_bank[c] is not None:
                        ge(pe, *wait_bank[c])
                    cs = slice(c * P, (c + 1) * P)
                    first, last = k == 0, k == ktot - 1
                    kk = k - k0
                    if token_major:
                        ps = bank[banks[c]][:, 0:CW]
                        t_.matmul(ps, xs[:, k, 0, cs], whi[s][:, kk, :], start=first, stop=False)
                        t_.matmul(ps, xs[:, k, 0, cs], wlo[s][:, kk, :], start=False, stop=False)
                        mm = t_.matmul(ps, xs[:, k, 1, cs], whi[s][:, kk, :], start=False,
                                       stop=last)
                    else:
                        mm = three(bank[banks[c]][:, 0:S], whi[s][:, kk, cs], wlo[s][:, kk, cs],
                                   xs[:, k, 0, :], xs[:, k, 1, :], first, last)
                    if (k, c) == order[-1]:
                        mm.then_inc(w_used[s], 1)
                    elif last:
                        mm.then_inc(tile_done, 1)

            def sums(s, b, tokens):
                pe.wait_ge(acc_done, 8 * (s + 1))
                mm = t_.matmul(bank[b][:, 0:S], ones[:], acc[:, :], start=True, stop=True)
                if tokens:
                    for tt in range(NT):
                        mm = t_.matmul(bank[b][:, S + tt:S + tt + 1], acc[:, tt * P:(tt + 1) * P],
                                       ones[:, 0:1], start=True, stop=True)
                mm.then_inc(ss_done, 1)

            pe.wait_ge(consts, 10)
            pe.wait_ge(v_in, 16 * 12)
            for n in range(5):
                r = 56 if n == 0 else 88
                dst = bank[7][:, n * P:n * P + r] if n < 4 else bank[2][:, 0:r]
                t_.transpose(dst, vrows[0:r, n, :], ident[0:r, 0:r]).then_inc(vt_done, 1)
            pe.wait_ge(x_in, 16)
            for q in range(4):
                for c in range(2):
                    for tt in range(NT):
                        k = 2 * q + c
                        mm = t_.transpose(bank[3 + q][:, c * S + tt * P:c * S + (tt + 1) * P],
                                          xtm[:, tt, k * P:(k + 1) * P], ident[:])
                mm.then_inc(xt_done, 1)
            pe.wait_ge(c_in, 64)
            t_.matmul(bank[1][0:NG * BH, 0:DIST], rb[:, :], oh[:, :], start=True, stop=False)
            t_.matmul(bank[1][0:NG * BH, 0:DIST], gs[:, :], mk[:, :], start=False, stop=True)\
                .then_inc(bt_done, 1)

            for u in range(12):
                t = 2 * u
                waits = [(ev_done, t + c - 2) for c in range(2)] if u else [None, (bt_copied, 1)]
                unit(U_IN + u, xsA, [t % 3, (t + 1) % 3], wait_bank=waits,
                     k_wait=(lambda k: pe.wait_ge(xlo_done, k + 1)) if u == 0 else None,
                     token_major=4 <= u < 8)
                if u == 0:
                    sums(0, 7, True)
                if u == 3:
                    pe.wait_ge(g_in, 32)
                    pe.wait_ge(xg_done, KD)
                    for j in range(2):
                        for k in range(KD):
                            mm = t_.matmul(bank[3][0:AH, j * S:(j + 1) * S],
                                           wg[:, k, j * AH:(j + 1) * AH], XG[:, k, :],
                                           start=k == 0, stop=k == KD - 1)
                    mm.then_inc(gates_ps, 1)
                if u == 6:
                    pe.wait_ge(gates_done, 1)
                    for st in range(NT):
                        mm = t_.transpose(bank[4][:, st * AH:(st + 1) * AH],
                                          gc[:, st * P:(st + 1) * P], ident[0:AH, 0:AH])
                    mm.then_inc(ct_done, 1)
                    for h in range(AH):
                        t_.matmul(bank[5 + h // 2][:, (h % 2) * S:(h % 2 + 1) * S], sel[:, h, :],
                                  gm[:, :], start=True, stop=True).then_inc(mb_done, 1)
                    for h in range(AH):
                        mm = t_.matmul(bank[(3, 7)[h // 2]][:, (h % 2) * S:(h % 2 + 1) * S],
                                       sel[:, h, :], gx[:, :], start=True, stop=True)
                        if h % 2:
                            mm.then_inc(eb_done, 1)
                if u == 7:
                    pe.wait_ge(ev_done, 8)
                    pe.wait_ge(ee_done, 2 * AH)
                    pe.wait_ge(eb_copied, 2)
                    for h in range(AH):
                        b = bank[3 + h]
                        t_.matmul(b[:, 0:S], kT[:, h, 0:P], qT[:, h, :], start=True, stop=True)
                        t_.matmul(b[:, S:384], kT[:, h, P:S], qT[:, h, P:S], start=True, stop=True)\
                            .then_inc(s_done, 1)
                if u in (8, 9):
                    pe.wait_ge(ev_done, 16)
                    for h in (0, 1) if u == 8 else (2, 3):
                        b = bank[3 + h]
                        pe.wait_ge(sd_done, h + 1)
                        ge(pe, den_abs, h)
                        t_.matmul(bank[7][:, 0:S], ones[:], SD[:, h, 0:S], start=True, stop=False)
                        t_.matmul(bank[7][:, P:S], ones[:], SD[:, h, S:384], start=False, stop=True)\
                            .then_inc(den_done, 1)
                        for c in range(2):
                            cs = slice(h * DV + c * P, h * DV + (c + 1) * P)
                            t_.matmul(b[:, c * S:(c + 1) * S], Vm[:, 0, cs], SD[:, h, 0:S],
                                      start=True, stop=False)
                            mm = t_.matmul(b[:, c * S + P:(c + 1) * S], Vm[:, 1, cs],
                                           SD[:, h, S:384], start=False, stop=True)
                        mm.then_inc(num_done, 1)
                if u == 10:
                    for h in range(AH):
                        pe.wait_ge(hsq_done, h + 1)
                        ps = bank[3 + h // 2][:, (h % 2) * S:(h % 2 + 1) * S]
                        t_.matmul(ps, ones[:], hsq[:, h, 0, :], start=True, stop=False)
                        mm = t_.matmul(ps, ones[:], hsq[:, h, 1, :], start=False, stop=True)
                        if h % 2:
                            mm.then_inc(hss_done, 1)

            def outproj(u0, e0, xs, k_wait, q0):
                pe.wait_ge(ev_done, e0)
                for u in range(4):
                    unit(u0 + u, xs, [0, 1],
                         wait_bank=[(x_new, q0 + 2 * u + c - 1) for c in range(2)] if u else (),
                         k_wait=None if u else k_wait)

            def ffn(u_up, e_up, u_down, p0, xs, x0, q0, s):
                def pair(n, p, i, step, first):
                    for g in range(2):
                        if first:
                            waits = [(x_new, q0 - 1 + c) for c in range(2)] if g else ()
                        else:
                            waits = [(ev_done, 4 * p + (e_up - 4 + 2 * g + c + 1)) for c in range(2)]
                        unit(n + g, xs, FB[2 * g:2 * g + 2], i, step, wait_bank=waits,
                             k_wait=(lambda k: pe.wait_ge(xlo_done, x0 + k + 1))
                             if first and not g else None)
                        if first and not g:
                            sums(s, 6, False)

                pair(u_up, 0, 0, 0, True)
                with pe.Fori(0, 3) as i:
                    for j in range(3):
                        pair(u_up + 2 + 2 * j, i * 3 + (1 + j), i, 6, False)
                pair(u_up + 20, PAIRS - 1, 0, 0, False)
                with pe.Fori(0, 4) as i:
                    for j, ks in enumerate(DOWN_K):
                        pe.wait_ge(hlo_done, p0 + ks[1] // 2)
                        unit(u_down + j, hs, [4, 5], i, 3, ks, KF,
                             wait_bank=[(x_new, i * 2 + (q0 + c - 1)) for c in range(2)]
                             if j == 0 else ())

            outproj(U_AOUT, E_UP0, xsB, lambda k: pe.wait_ge(mlo_done, k + 1), 8)
            ffn(U_UP0, E_UP0, U_DOWN0, 0, xsA, 8, 16, 1)

            sums(2, 7, True)
            pe.wait_ge(xlo_done, 32)
            with pe.Fori(0, NHB) as i:
                def qkv(u):
                    t = 2 * u
                    unit(U_QKV + u, xsB if u in (0, 2, 4) else xsA, [t % 3, (t + 1) % 3], i, 9,
                         wait_bank=[(ev_done, i * 18 + (E_QKV + t + c - 2)) for c in range(2)],
                         token_major=u >= 6)

                def half(u, c):
                    n, t = U_QKV + u, 2 * u + c
                    s = n % RING
                    if c == 0:
                        pe.wait_ge(lo_done[s], rnd(n, i, 9) + 1)
                    pe.wait_ge(ev_done, i * 18 + (E_QKV + t - 2))
                    cs = slice(c * P, (c + 1) * P)
                    ps = bank[t % 3][:, 0:CW]
                    for k in range(KD):
                        t_.matmul(ps, xsA[:, k, 0, cs], whi[s][:, k, :], start=k == 0, stop=False)
                        t_.matmul(ps, xsA[:, k, 0, cs], wlo[s][:, k, :], start=False, stop=False)
                        mm = t_.matmul(ps, xsA[:, k, 1, cs], whi[s][:, k, :], start=False,
                                       stop=k == KD - 1)
                    mm.then_inc(w_used[s] if c else tile_done, 1)

                def scores(s):
                    h, tt = divmod(s, 2)
                    rows = slice((h % 2) * DH, (h % 2 + 1) * DH)
                    w = P * (1 + tt)
                    if s == 0:
                        pe.wait_ge(ev_done, i * 18 + (E_QKV + 12))
                    else:
                        pe.wait_ge(smax_done, i * 8 + s)
                    for g in range(NG):
                        mm = t_.matmul(two[0][:, g * w:(g + 1) * w],
                                       QT[rows, g, h // 2, tt * P:(tt + 1) * P],
                                       KT[rows, g, h // 2, 0:w], start=True, stop=True)
                    mm.then_inc(sc_done, 1)

                def turned(s):
                    tt = s % 2
                    pe.wait_ge(exp_done, i * 8 + (s + 1))
                    if s:
                        pe.wait_ge(pt_done, i * 8 + s)
                    for b in range(NG * (1 + tt)):
                        mm = t_.transpose(two[1][:, b * P:(b + 1) * P],
                                          SB[:, s % 2, b * P:(b + 1) * P], ident[:])
                    mm.then_inc(tr_done, 1)

                def mixed(h):
                    pe.wait_ge(pt_done, i * 8 + (2 * h + 2))
                    if h:
                        pe.wait_ge(o_done, i * 8 + 2 * h)
                    else:
                        pe.wait_ge(ev_done, i * 18 + (E_QKV + 18))
                    if h == 2:
                        pe.wait_ge(alo_done, i * 2 + 1)
                    for tt in range(NT):
                        blocks = [(g, 0, g) for g in range(NG)] if tt == 0 else \
                            [(g, kt, 3 + 2 * g + kt) for g in range(NG) for kt in range(NT)]
                        for m, (g, kt, b) in enumerate(blocks):
                            mm = t_.matmul(bank[7][:, tt * DH:(tt + 1) * DH], PT[:, h, b, :],
                                           Va[:, kt, g, h * DH:(h + 1) * DH], start=m == 0,
                                           stop=m == len(blocks) - 1)
                    mm.then_inc(pv_done, 1)

                def flipped(c):
                    pe.wait_ge(o_done, i * 8 + (4 * c + 4))
                    for tt in range(NT):
                        mm = t_.matmul(bank[7][:, S + tt * P:S + (tt + 1) * P],
                                       ohb[:, tt, c * P:(c + 1) * P], anti[:], start=True, stop=True)
                    mm.then_inc(flip_done, 1)

                for u in range(6):
                    qkv(u)
                scores(0)
                for m in range(6):
                    half(6 + m // 2, m % 2)
                    turned(m)
                    scores(m + 1)
                mixed(0)
                turned(6)
                scores(7)
                mixed(1)
                flipped(0)
                mixed(2)
                turned(7)
                mixed(3)
                flipped(1)

            outproj(U_BOUT, E_UP1, aTs, lambda k: pe.wait_ge(alo_done, k + 1), 24)
            ffn(U_UP1, E_UP1, U_DOWN1, PAIRS, xsB, 32, 32, 3)
            sums(4, 6, False)
            for m in range(8):
                tt, q = divmod(m, 4)
                for c in range(2):
                    k = 2 * q + c
                    pe.wait_ge(yn_done, k + 1)
                    if m >= 4:
                        pe.wait_ge(ytm_done, m - 3)
                    mm = t_.transpose(bank[m % 4][:, c * P:(c + 1) * P],
                                      Y[:, k, tt * P:(tt + 1) * P], ident[:])
                mm.then_inc(yt_done, 1)


NAMES = ("x", "a_norm_g", "a_w_in", "a_b_if", "a_hnorm_g", "a_w_out", "kv_norm_g", "w_kv",
         "b_norm_g", "b_w_q", "b_w_out", "rel_bias", "f_norm_g", "f_w_up", "f_conv_w", "f_conv_b",
         "f_w_down", "final_norm_g")


def kernel(**inputs):
    import concourse.bacc as bacc
    from concourse.bass_utils import run_bass_kernel_spmd

    nc = bacc.Bacc("TRN2", target_bir_lowering=False, num_devices=1)
    arrays = {n: np.ascontiguousarray(inputs[n]) for n in NAMES}
    arrays.update(zip(("onehot", "mask", "group"), distance_tables()))
    args = [nc.dram_tensor(f"in_{n}", a.shape, mybir.dt.from_np(a.dtype), kind="ExternalInput").ap()
            for n, a in arrays.items()]
    out = nc.dram_tensor("out", (1, S, D), F32, kind="ExternalOutput").ap()
    build(nc, *args, out)
    r = run_bass_kernel_spmd(nc, [{f"in_{n}": a for n, a in arrays.items()}], core_ids=[0])
    return r.results[0]["out"]
```

```python
from contextlib import ExitStack

import concourse.bass as bass
import numpy as np
from concourse import mybir

P = 128
D = 1024
S = 256
KD = D // P
NT = S // P
CW = 256
SLOT = KD * CW
RING = 3
AH, DK, DV = 4, 128, 256
FF = 2816
KF = FF // P
PAIRS = FF // CW
NG, BH, DH = 3, 16, 64
HB = CW // DH
NHB = BH // HB
EPS = 1e-6
CAP = 15.0
BUCKETS, MAXD = 32, 2048
GROUPS = ((128, 1), (512, 4), (2048, 16))
DIST = 384
MASKED = -1e30

DOWN_K = ((0, 8), (8, 16), (16, 22))
U_IN, U_AOUT = 0, 12
U_UP0, U_DOWN0 = 16, 38
U_QKV, U_BOUT = 50, 86
U_UP1, U_DOWN1 = 90, 112
U_END = 124
T_IN, T_AOUT = 0, 12
T_UP0, T_DOWN0 = 16, 38
T_QKV, T_BOUT = 42, 78
T_UP1, T_DOWN1 = 82, 104
E_UP0, E_QKV, E_UP1, E_END = 24, 68, 140, 184
FB = (2, 3, 0, 1)
V_A, V_KV, V_B, V_F0, V_F1, V_FIN, V_HN = range(0, 56, 8)
V_CONV = 56
V_END = V_CONV + 2 * 4 * 2 * KF
BODY = (("q", 1), ("k", 1), ("q", 2), ("k", 2), ("v", 0), ("v", 1), ("v", 2), ("q", 0), ("k", 0))
U_BODY = 52

F32 = mybir.dt.float32
F32R = mybir.dt.float32r
ALU = mybir.AluOpType
ACT = mybir.ActivationFunctionType


def distance_tables():
    dist = 255 - np.arange(DIST)
    exact = BUCKETS // 2
    d = np.maximum(dist, 0)
    ratio = np.log(np.maximum(d, 1) / exact) / np.log(MAXD / exact)
    large = np.minimum(exact + (ratio * (BUCKETS - exact)).astype(np.int64), BUCKETS - 1)
    bucket = np.where(d < exact, d, large)
    onehot = (bucket[None, :] == np.arange(BUCKETS)[:, None]).astype(np.float32)
    mask = np.stack([np.where((dist >= 0) & (dist % dil == 0) & (dist <= win), 0.0, MASKED)
                     for win, dil in GROUPS]).astype(np.float32)
    group = np.repeat(np.eye(NG, dtype=np.float32), BH, axis=1)
    return onehot, mask, group


def build(nc, xT, vectors, b_if, a_w_in, a_w_out, w_kv, b_w_q, b_w_out, rel_bias, f_w_up,
          f_w_down, onehot, mask, group, out):
    ctx = ExitStack()
    with ctx:
        sems = {}

        def sem(name):
            sems[name] = ctx.enter_context(nc.semaphore(name))
            return sems[name]

        at = [(int(nc.sbuf_base) + 63) // 64 * 64]

        def place(name, shape, dt=F32, arena=None):
            cur = at if arena is None else arena
            n = 4
            for s in shape[1:]:
                n *= s
            t = nc.alloc_sbuf_tensor_at(name, shape, dt, offset=cur[0])
            cur[0] += (n + 63) // 64 * 64
            return t

        raw = [place(f"raw{s}", [P, SLOT]) for s in range(RING)]
        whi = [place(f"whi{s}", [P, KD, CW], F32R) for s in range(RING)]
        wlo = [place(f"wlo{s}", [P, KD, CW], F32R) for s in range(RING)]
        X = place("X", [P, KD, S])
        xsA = place("xsA", [P, KD, 2, S], F32R)
        xsB = place("xsB", [P, KD, 2, S], F32R)
        ident = place("ident", [P, P])
        anti = place("anti", [P, P])
        ones = place("ones", [P, P])
        sel = place("sel", [AH, AH, P])
        vcols = place("vcols", [P, V_END])
        acc = place("acc", [P, S])
        sq = place("sq", [P, 2, S])
        root = place("root", [P, S + NT])
        rstd = place("rstd", [P, S + NT])
        bif = place("bif", [AH, 2])
        epsc = place("epsc", [P, 1])
        onec = place("onec", [P, 1])
        wroot = place("wroot", [P, 1])
        bv = place("bv", [NG * BH, DIST])
        oh = place("oh", [BUCKETS, DIST])
        mk = place("mk", [NG, DIST])
        gs = place("gs", [NG, NG * BH])
        rb = place("rb", [BUCKETS, NG * BH])
        base = at[0]

        ar = [base]
        hm = place("hm", [P, AH, 2, S], F32, ar)
        hsq = place("hsq", [P, AH, 2, S], F32, ar)
        wg = place("wg", [P, KD, 2 * AH], F32, ar)
        wgh = place("wgh", [P, KD, 2 * AH], F32R, ar)
        wgl = place("wgl", [P, KD, 2 * AH], F32R, ar)
        gtm = place("gtm", [P, NT, 2 * AH], F32, ar)
        qT = place("qT", [P, AH, S], F32, ar)
        kT = place("kT", [P, AH, S], F32, ar)
        Vm = place("Vm", [P, NT, AH * DV], F32, ar)
        sig = place("sig", [P, KD, S], F32, ar)
        gz = place("gz", [AH, 2, S], F32, ar)
        gt = place("gt", [AH, 2, S], F32, ar)
        gp = place("gp", [AH, S], F32, ar)
        gl = place("gl", [AH, S], F32, ar)
        gn = place("gn", [AH, S], F32, ar)
        gc = place("gc", [AH, S], F32, ar)
        gm = place("gm", [AH, S], F32, ar)
        gd = place("gd", [AH, S], F32, ar)
        gx = place("gx", [AH, S], F32, ar)
        gones = place("gones", [AH, S], F32, ar)
        cS = place("cS", [P, NT, AH], F32, ar)
        EE = place("EE", [P, AH, 384], F32, ar)
        SD = place("SD", [P, AH, 384], F32, ar)
        EB = place("EB", [P, AH, S], F32, ar)
        den = place("den", [P, AH, S], F32, ar)
        dinv = place("dinv", [P, AH, S], F32, ar)
        assert ar[0] <= nc.sbuf_usable_end, ar[0]
        hroot = place("hroot", [P, AH, S], F32, [base + 2 * 8192 + 4 * 256])
        hrs = place("hrs", [P, AH, S], F32, [base + 2 * 8192 + 4 * 256 + 4096])

        ar = [base]
        hs = place("hs", [P, KF, 2, S], F32R, ar)
        ub = place("ub", [P, 4, S + 2], F32, ar)
        cb = place("cb", [P, 4, S], F32, ar)
        gb = place("gb", [P, 2, S], F32, ar)
        hb_ = place("hb", [P, 2, S], F32, ar)
        ar = [base]
        QT = place("QT", [P, NG, 2, S], F32, ar)
        KT = place("KT", [P, NG, 2, S], F32, ar)
        Va = place("Va", [P, NT, NG, CW], F32, ar)
        PT = place("PT", [P, HB, 9, P], F32, ar)
        Bi = place("Bi", [P, HB, NG, S], F32, ar)
        SB = place("SB", [P, 2, NG * S], F32, ar)
        ohb = place("ohb", [P, NT, CW], F32, ar)
        aTs = place("aTs", [P, KD, 2, S], F32R, ar)
        nmx = place("nmx", [P, 2 * HB], F32, ar)
        mxx = place("mxx", [P, 2 * HB], F32, ar)
        lsum = place("lsum", [P, 2 * HB], F32, ar)
        linv = place("linv", [P, 2 * HB], F32, ar)
        carry = place("carry", [P, 2], F32, ar)
        assert ar[0] <= nc.sbuf_usable_end, ar[0]
        ar = [base]
        Y = place("Y", [P, KD, S], F32, ar)
        assert at[0] <= nc.sbuf_usable_end

        bank = [ctx.enter_context(nc.psum_tensor(f"bank{b}", [P, 512], F32)) for b in range(3)]
        two = [ctx.enter_context(nc.psum_tensor(f"banks{b}", [P, 1024], F32)) for b in (34, 56)]
        bank += [two[0][:, 0:512], two[0][:, 512:1024], two[1][:, 0:512], two[1][:, 512:1024]]
        bank.append(ctx.enter_context(nc.psum_tensor("bank7", [P, 512], F32)))

        bvd = nc.dram_tensor("bias_by_distance", (NG * BH, DIST), F32, kind="Internal")

        raw_in = [sem(f"raw_in{s}") for s in range(RING)]
        hi_done = [sem(f"hi_done{s}") for s in range(RING)]
        lo_done = [sem(f"lo_done{s}") for s in range(RING)]
        w_used = [sem(f"w_used{s}") for s in range(RING)]
        x_in = [sem("x_in0"), sem("x_in1")]
        v_in, c_in, g_in = sem("v_in"), sem("c_in"), sem("g_in")
        bv_out, bi_in, y_out = sem("bv_out"), [sem(f"bi_in{h}") for h in range(HB)], sem("y_out")
        consts = sem("consts")
        bt_done, bt_copied = sem("bt_done"), sem("bt_copied")
        tile_done = sem("tile_done")
        ev_done = sem("ev_done")
        x_new = sem("x_new")
        sq_done = sem("sq_done")
        acc_zero = sem("acc_zero")
        acc_done = sem("acc_done")
        xhi_done = sem("xhi_done")
        xlo_done = sem("xlo_done")
        warm = sem("warm")
        ss_done = sem("ss_done")
        root_done, rstd_done = sem("root_done"), sem("rstd_done")
        wgh_done, wgl_done, gtm_done = sem("wgh_done"), sem("wgl_done"), sem("gtm_done")
        gtt_done = sem("gtt_done")
        gates_ps, gseq, gact = sem("gates_ps"), sem("gseq"), sem("gact")
        gates_done = sem("gates_done")
        ct_done, mb_done, eb_done = sem("ct_done"), sem("mb_done"), sem("eb_done")
        cs_done, eb_copied = sem("cs_done"), sem("eb_copied")
        ee_done, dm_exp, dm_done = sem("ee_done"), sem("dm_exp"), sem("dm_done")
        s_done, sd_done = sem("s_done"), sem("sd_done")
        den_done, den_abs, dmax_done, dinv_done = (sem("den_done"), sem("den_abs"),
                                                   sem("dmax_done"), sem("dinv_done"))
        num_done, hm_done, hsq_done = sem("num_done"), sem("hm_done"), sem("hsq_done")
        hss_done, hroot_done, hrs_done = sem("hss_done"), sem("hroot_done"), sem("hrs_done")
        sig_done, hn_done, hg_done = sem("sig_done"), sem("hn_done"), sem("hg_done")
        mhi_done, mlo_done = sem("mhi_done"), sem("mlo_done")
        pad_done = sem("pad_done")
        t1_done, cA_done, cB_done = sem("t1_done"), sem("cA_done"), sem("cB_done")
        silu_done, mul_done = sem("silu_done"), sem("mul_done")
        hhi_done, hlo_done = sem("hhi_done"), sem("hlo_done")
        sc_done, smax_done, nmx_done = sem("sc_done"), sem("smax_done"), sem("nmx_done")
        exp_done, tr_done, pt_done = sem("exp_done"), sem("tr_done"), sem("pt_done")
        pv_done, linv_done, o_done = sem("pv_done"), sem("linv_done"), sem("o_done")
        flip_done, ahi_done, alo_done = sem("flip_done"), sem("ahi_done"), sem("alo_done")
        yn_done = sem("yn_done")

        block = ctx.enter_context(nc.Block())

        def rnd(n, i=0, step=0):
            return n // RING + i * (step // RING) if step else n // RING

        def ge(eng, s, v):
            if not (isinstance(v, int) and v <= 0):
                eng.wait_ge(s, v)

        def col(c):
            return vcols[:, c:c + 1]

        def conv_col(layer, tap, ch):
            return vcols[:, bass.ds(ch + (V_CONV + (4 * layer + tap) * 2 * KF), 1)]

        @block.sync
        def _(sp):
            def load(n, i, step, src, nk):
                s = n % RING
                if n >= RING:
                    sp.wait_ge(lo_done[s], rnd(n, i, step))
                sp.dma_start(raw[s][:, 0:nk * CW].rearrange("p (k c) -> p k c", c=CW),
                             src).then_inc(raw_in[s], 16)

            def cols(w, c):
                return w.rearrange("(k p) n -> p k n", p=P)[:, :, bass.ds(c, CW)]

            w_in = a_w_in[0]
            for u in range(12):
                load(U_IN + u, 0, 0, cols(w_in, u * CW), KD)
                if u == 0:
                    for half in range(2):
                        ks = slice(4 * half, 4 * half + 4)
                        sp.dma_start(X[:, ks, :], xT[:, ks, :]).then_inc(x_in[half], 16)
            for u in range(4):
                load(U_AOUT + u, 0, 0, cols(a_w_out[0], u * CW), KD)

            def ffn(layer, u_up, u_down):
                w = f_w_up[layer]

                def pair(n, i, step, p):
                    load(n, i, step, cols(w, p * CW), KD)
                    load(n + 1, i, step, cols(w, p * CW + FF), KD)

                pair(u_up, 0, 0, 0)
                with sp.Fori(0, 3) as i:
                    for j in range(3):
                        pair(u_up + 2 + 2 * j, i, 6, i * 3 + (1 + j))
                pair(u_up + 20, 0, 0, PAIRS - 1)
                wd = f_w_down[layer].rearrange("(k p) n -> p k n", p=P)
                with sp.Fori(0, 4) as i:
                    for j, (k0, k1) in enumerate(DOWN_K):
                        load(u_down + j, i, 3, wd[:, k0:k1, bass.ds(i * CW, CW)], k1 - k0)

            ffn(0, U_UP0, U_DOWN0)
            def block_unit(n, i, step, hb, kind, g):
                w = b_w_q[0] if kind == "q" else w_kv
                load(n, i, step, cols(w, hb * CW + (g + NG * (kind == "v")) * D), KD)

            block_unit(U_QKV, 0, 0, 0, "q", 0)
            block_unit(U_QKV + 1, 0, 0, 0, "k", 0)
            with sp.Fori(0, NHB - 1) as i:
                for j, (kind, g) in enumerate(BODY):
                    block_unit(U_BODY + j, i, 9, i + 1 if j >= 7 else i, kind, g)
            for j, (kind, g) in enumerate(BODY[:7]):
                block_unit(U_BODY + 27 + j, 0, 0, NHB - 1, kind, g)
            for u in range(4):
                load(U_BOUT + u, 0, 0, cols(b_w_out[0], u * CW), KD)
            ffn(1, U_UP1, U_DOWN1)
            for q in range(4):
                sp.wait_ge(yn_done, 2 * q + 2)
                sp.dma_start(out[:, 2 * q:2 * q + 2, :], Y[:, 2 * q:2 * q + 2, :])\
                    .then_inc(y_out, 16)
            sp.wait_ge(y_out, 16 * 4)
            sp.wait_ge(bv_out, 16)

        @block.gpsimd
        def _(pool):
            g = nc.gpsimd
            g.memset(ident[:], 0.0).then_inc(consts, 1)
            g.memset(anti[:], 0.0).then_inc(consts, 1)
            g.memset(sel[:], 0.0).then_inc(consts, 1)
            g.memset(ones[:], 1.0).then_inc(consts, 1)
            g.memset(epsc[:], EPS).then_inc(consts, 1)
            g.memset(onec[:], 1.0).then_inc(consts, 1)
            g.memset(gones[:], 1.0).then_inc(consts, 1)
            pool.wait_ge(consts, 7)
            g.affine_select(out=ident[:], in_=ident[:], compare_op=ALU.not_equal, fill=1.0, base=0,
                            pattern=[[-1, P]], channel_multiplier=1).then_inc(consts, 1)
            g.affine_select(out=anti[:], in_=anti[:], compare_op=ALU.not_equal, fill=1.0,
                            base=-(P - 1), pattern=[[1, P]], channel_multiplier=1).then_inc(consts, 1)
            g.affine_select(out=sel[:], in_=sel[:], compare_op=ALU.not_equal, fill=1.0, base=0,
                            pattern=[[-1, AH], [0, P]], channel_multiplier=1).then_inc(consts, 1)

            def lo(n, i=0, step=0):
                s = n % RING
                pool.wait_ge(hi_done[s], rnd(n, i, step) + 1)
                g.tensor_tensor(wlo[s][:, :, :], raw[s][:, :].rearrange("p (k c) -> p k c", c=CW),
                                whi[s][:, :, :].bitcast(F32), ALU.subtract).then_inc(lo_done[s], 1)

            for n in range(U_IN, 6):
                if n % RING:
                    lo(n)
            pool.wait_ge(dm_exp, 2 * AH)
            g.affine_select(out=EE[:, :, 0:S], in_=EE[:, :, 0:S], compare_op=ALU.is_ge, fill=0.0,
                            base=0, pattern=[[0, AH], [1, S]], channel_multiplier=-1)\
                .then_inc(dm_done, 1)
            g.affine_select(out=EE[:, :, S:384], in_=EE[:, :, S:384], compare_op=ALU.is_ge,
                            fill=0.0, base=0, pattern=[[0, AH], [1, P]], channel_multiplier=-1)\
                .then_inc(dm_done, 1)
            with pool.Fori(0, (U_END - 7) // RING) as i:
                for n in (7, 8):
                    lo(n, i, RING)

        @block.scalar
        def _(act):
            a = nc.scalar

            def hi(n, i=0, step=0):
                s = n % RING
                act.wait_ge(raw_in[s], (rnd(n, i, step) + 1) * 16)
                if n >= RING:
                    act.wait_ge(w_used[s], rnd(n, i, step))
                a.activation(whi[s][:, :, :], raw[s][:, :].rearrange("p (k c) -> p k c", c=CW),
                             ACT.Copy).then_inc(hi_done[s], 1)

            def post(k, q, sets, i=0, dq=0):
                if q < KD:
                    act.wait_ge(x_in[k // 4], 16)
                else:
                    act.wait_ge(x_new, q + i * dq + (1 - KD))
                if q >= 2:
                    act.wait_ge(acc_done, q + i * dq - 1)
                for dst, gain in sets:
                    a.activation(dst[:, bass.ds(k, 1), 0, :], X[:, bass.ds(k, 1), :], ACT.Copy,
                                 scale=vcols[:, bass.ds(k + gain, 1)]).then_inc(xhi_done, 1)
                a.activation(sq[:, q % 2, :], X[:, bass.ds(k, 1), :].rearrange("p a t -> p (a t)"),
                             ACT.Square).then_inc(sq_done, 1)

            def warm_root():
                a.activation(wroot[:, :], epsc[:, :], ACT.Sqrt).then_inc(warm, 1)

            def root_of(s, width, b):
                act.wait_ge(ss_done, s + 1)
                if s:
                    act.wait_ge(rstd_done, s)
                a.activation(root[:, 0:width], bank[b][:, 0:width], ACT.Sqrt, bias=epsc[:, 0:1],
                             scale=1.0 / D).then_inc(root_done, 1)

            def gate(k):
                act.wait_ge(ev_done, 16 + k + 1)
                a.activation(sig[:, k, :], sig[:, k, :], ACT.Sigmoid).then_inc(sig_done, 1)

            def m_hi(k):
                act.wait_ge(hg_done, k + 1)
                a.activation(xsB[:, k, 0, :], hm[:, k // 2, k % 2, :], ACT.Copy)\
                    .then_inc(mhi_done, 1)

            act.dma_start(vcols[:, :], vectors).then_inc(v_in, 16)
            act.dma_start(wg[:, :, :], a_w_in[0].rearrange("(k p) n -> p k n", p=P)
                          [:, :, 12 * CW:12 * CW + 2 * AH]).then_inc(g_in, 16)
            act.dma_start(bif[:, :], b_if).then_inc(g_in, 16)
            act.dma_start(oh[:], onehot).then_inc(c_in, 16)
            act.dma_start(mk[:], mask).then_inc(c_in, 16)
            act.dma_start(gs[:], group).then_inc(c_in, 16)
            act.dma_start(rb[:], rel_bias).then_inc(c_in, 16)

            act.wait_ge(consts, 10)
            warm_root()
            hi(0)
            act.wait_ge(v_in, 16)
            for k in range(KD):
                post(k, k, ((xsA, V_A),))
            hi(1)
            root_of(0, S + NT, 7)
            hi(2)
            act.wait_ge(g_in, 32)
            a.activation(wgh[:, :, :], wg[:, :, :], ACT.Copy).then_inc(wgh_done, 1)
            for u in range(12):
                if u == 3:
                    act.wait_ge(gseq, 2)
                    a.activation(gt[:, :, :], gz[:, :, :], ACT.Tanh, scale=1.0 / CAP).then_inc(gact, 1)
                    act.wait_ge(gact, 1)
                    a.activation(gp[:, :], gt[:, 1, :], ACT.Exp, scale=-CAP).then_inc(gact, 1)
                    act.wait_ge(gact, 2)
                    a.activation(gl[:, :], gp[:, :], ACT.Ln, bias=onec[0:AH, 0:1])\
                        .then_inc(gact, 1)
                    act.wait_ge(bt_copied, 1)
                    act.dma_start(bvd.ap(), bv[:, :]).then_inc(bv_out, 16)
                    act.wait_ge(gseq, 6)
                    a.activation(gx[:, :], gd[:, :], ACT.Exp).then_inc(gates_done, 1)
                if u == 5:
                    for b in range(2):
                        act.wait_ge(eb_done, b + 1)
                        a.activation(EB[:, 2 * b:2 * b + 2, :],
                                     bank[(3, 7)[b]][:, :].rearrange("p (h t) -> p h t", h=2),
                                     ACT.Copy).then_inc(eb_copied, 1)
                    for e in range(2 * AH):
                        h, st = divmod(e, 2)
                        c = slice(0, S) if st == 0 else slice(S, 384)
                        act.wait_ge(ee_done, e + 1)
                        a.activation(EE[:, h, c], EE[:, h, c], ACT.Exp, scale=-1.0)\
                            .then_inc(dm_exp, 1)
                for h in {7: (0, 1), 8: (2,), 9: (3,)}.get(u, ()):
                    act.wait_ge(den_done, h + 1)
                    a.activation(den[:, h, :], bank[7][:, 0:S], ACT.Abs).then_inc(den_abs, 1)
                    act.wait_ge(hm_done, h + 1)
                    a.activation(hsq[:, h, :, :], hm[:, h, :, :], ACT.Square).then_inc(hsq_done, 1)
                if u in (8, 10):
                    b = u // 10
                    act.wait_ge(hss_done, b + 1)
                    a.activation(hroot[:, 2 * b:2 * b + 2, :],
                                 bank[3 + b][:, :].rearrange("p (h t) -> p h t", h=2),
                                 ACT.Sqrt, bias=epsc[:, 0:1], scale=1.0 / DV)\
                        .then_inc(hroot_done, 1)
                if u == 11:
                    for k in range(6):
                        gate(k)
                    for k in range(4):
                        m_hi(k)
                hi(u + 3)
            for k in (6, 7):
                gate(k)
            for k in range(4, KD):
                m_hi(k)
            for u in range(4):
                if u == 3:
                    warm_root()
                for c in range(2):
                    k = 2 * u + c
                    post(k, 8 + k, ((xsA, V_F0),))
                hi(U_AOUT + u + 3)

            def ffn(layer, u_up, e_up, u_down, q0, sets, s):
                f0, p0 = 4 * PAIRS * layer, PAIRS * layer

                def first_tap(p, g):
                    for c in range(2):
                        j = 2 * g + c
                        act.wait_ge(ev_done, 4 * p + (e_up + j + 1))
                        ge(act, mul_done if g else silu_done, p + p0)
                        ch = p * 2 + (KF * g + c)
                        a.activation(cb[:, j, :], ub[:, j, 2:S + 2], ACT.Identity,
                                     scale=conv_col(layer, 2, ch), bias=conv_col(layer, 3, ch))\
                            .then_inc(t1_done, 1)

                def h_hi(p):
                    act.wait_ge(mul_done, p + (p0 + 1))
                    a.activation(hs[:, bass.ds(p * 2, 2), 0, :], hb_[:, :, :], ACT.Copy)\
                        .then_inc(hhi_done, 1)

                def pair(n, p, i, step, first):
                    if first:
                        root_of(s, S, 6)
                    hi(n + 3, i, step)
                    first_tap(p, 0)
                    if not first:
                        h_hi(p - 1)
                    hi(n + 4, i, step)
                    first_tap(p, 1)
                    act.wait_ge(cB_done, 4 * p + (f0 + 2))
                    ge(act, mul_done, p + p0)
                    a.activation(gb[:, :, :], cb[:, 0:2, :], ACT.Silu).then_inc(silu_done, 1)

                pair(u_up, 0, 0, 0, True)
                with act.Fori(0, 3) as i:
                    for j in range(3):
                        pair(u_up + 2 + 2 * j, i * 3 + (1 + j), i, 6, False)
                pair(u_up + 20, PAIRS - 1, 0, 0, False)
                h_hi(PAIRS - 1)
                with act.Fori(0, 3) as i:
                    hi(u_down + 3, i, 3)
                    hi(u_down + 4, i, 3)
                    for c in range(2):
                        post(i * 2 + c, q0 + c, sets, i, 2)
                    hi(u_down + 5, i, 3)
                for n in (12, 13):
                    if u_down + n < U_END:
                        hi(u_down + n)
                warm_root()
                for k in (6, 7):
                    post(k, q0 + k, sets)
                if u_down + 14 < U_END:
                    hi(u_down + 14)

            ffn(0, U_UP0, E_UP0, U_DOWN0, 16, ((xsA, V_KV), (xsB, V_B)), 1)

            def block(i, step, last):
                n0 = U_BODY + (27 if last else 0)
                hb = NHB - 1 if last else i
                for h in range(HB):
                    if h == 0:
                        act.wait_ge(bv_out, 16)
                    src = bass.AP(bvd, (hb * HB + h) * DIST, [[1, P], [BH * DIST, NG], [1, S]])
                    act.dma_start(Bi[:, h, :, :], src).then_inc(bi_in[h], 16)

                def soft(s):
                    h, tt = divmod(s, 2)
                    w = NG * P * (1 + tt)
                    act.wait_ge(nmx_done, hb * 8 + (s + 1))
                    a.activation(SB[:, s % 2, 0:w], SB[:, s % 2, 0:w], ACT.Exp,
                                 bias=nmx[:, s:s + 1], accum_out=lsum[:, s:s + 1])\
                        .then_inc(exp_done, 1)

                def a_hi(c):
                    act.wait_ge(flip_done, hb * 2 + (c + 1))
                    a.activation(aTs[:, bass.ds(hb * 2 + c, 1), 0, :], bank[3][:, 0:S]
                                 .rearrange("p (a t) -> p a t", a=1), ACT.Copy)\
                        .then_inc(ahi_done, 1)

                for j in range(4):
                    hi(n0 + j + 3, i, step)
                for m in range(3):
                    soft(2 * m)
                    soft(2 * m + 1)
                    hi(n0 + 4 + m + 3, i, step)
                soft(6)
                soft(7)
                if not last:
                    hi(n0 + 7 + 3, i, step)
                a_hi(0)
                if not last:
                    hi(n0 + 8 + 3, i, step)
                a_hi(1)

            hi(U_QKV + 3)
            root_of(2, S + NT, 7)
            hi(U_QKV + 4)
            with act.Fori(0, NHB - 1) as i:
                block(i, 9, False)
            block(0, 0, True)
            for u in range(4):
                if u == 3:
                    warm_root()
                for c in range(2):
                    k = 2 * u + c
                    post(k, 24 + k, ((xsB, V_F1),))
                hi(U_BOUT + u + 3)
            ffn(1, U_UP1, E_UP1, U_DOWN1, 32, (), 3)
            root_of(4, S, 6)

        @block.vector
        def _(dve):
            v = nc.vector

            def lo(n, i=0, step=0):
                if n % RING or n >= U_END:
                    return
                dve.wait_ge(hi_done[0], rnd(n, i, step) + 1)
                v.tensor_tensor(wlo[0][:, :, :], raw[0][:, :].rearrange("p (k c) -> p k c", c=CW),
                                whi[0][:, :, :].bitcast(F32), ALU.subtract).then_inc(lo_done[0], 1)

            def acc_clear(q):
                if q:
                    dve.wait_ge(ss_done, q // 8)
                v.memset(acc[:, :], 0.0).then_inc(acc_zero, 1)
                dve.wait_ge(acc_zero, q // 8 + 1)

            def post(k, q, x0, sets, i=0, dq=0):
                for m, (dst, gain) in enumerate(sets):
                    dve.wait_ge(xhi_done, x0 + m + 1 + i * (dq * len(sets)))
                    v.scalar_tensor_tensor(dst[:, bass.ds(k, 1), 1, :], X[:, bass.ds(k, 1), :],
                                           vcols[:, bass.ds(k + gain, 1)],
                                           dst[:, bass.ds(k, 1), 0, :].bitcast(F32),
                                           ALU.mult, ALU.subtract).then_inc(xlo_done, 1)
                dve.wait_ge(sq_done, q + i * dq + 1)
                ge(dve, acc_done, q + i * dq)
                v.tensor_tensor(acc[:, :], acc[:, :], sq[:, q % 2, :], ALU.add)\
                    .then_inc(acc_done, 1)

            def gated(k):
                dve.wait_ge(sig_done, k + 1)
                dve.wait_ge(hn_done, k // 2 + 1)
                hk = hm[:, k // 2, k % 2, :]
                v.scalar_tensor_tensor(hk, hk, col(V_HN + k), sig[:, k, :], ALU.mult, ALU.mult)\
                    .then_inc(hg_done, 1)

            def m_lo(k):
                dve.wait_ge(mhi_done, k + 1)
                v.tensor_tensor(xsB[:, k, 1, :], hm[:, k // 2, k % 2, :],
                                xsB[:, k, 0, :].bitcast(F32), ALU.subtract).then_inc(mlo_done, 1)

            def rstd_of(s, width):
                dve.wait_ge(root_done, s + 1)
                v.reciprocal(rstd[:, 0:width], root[:, 0:width]).then_inc(rstd_done, 1)
                dve.wait_ge(rstd_done, s + 1)

            def complete(c, m, n, i=0, step=0):
                if c:
                    dve.wait_ge(w_used[n % RING], rnd(n, i, step) + 1)
                else:
                    dve.wait_ge(tile_done, m + 1)

            def residual(k, c, m, n, b, i=0, step=0):
                complete(c, m, n, i, step)
                xk = X[:, bass.ds(k, 1), :].rearrange("p a t -> p (a t)")
                v.tensor_tensor(xk, xk, bank[b][:, 0:S], ALU.add).then_inc(x_new, 1)

            acc_clear(0)
            lo(0)
            dve.wait_ge(v_in, 16)
            for k in range(KD):
                dve.wait_ge(x_in[k // 4], 16)
                post(k, k, k, ((xsA, V_A),))
            rstd_of(0, S + NT)
            dve.wait_ge(wgh_done, 1)
            v.tensor_tensor(wgl[:, :, :], wg[:, :, :], wgh[:, :, :].bitcast(F32), ALU.subtract)\
                .then_inc(wgl_done, 1)
            for u in range(12):
                lo(u + 2)
                if u == 2:
                    dve.wait_ge(gates_ps, 1)
                    for tt in range(NT):
                        v.tensor_scalar(gtm[:, tt, :], bank[3][:, tt * 2 * AH:(tt + 1) * 2 * AH],
                                        rstd[:, S + tt:S + tt + 1], None, ALU.mult)\
                            .then_inc(gtm_done, 1)
                if u == 3:
                    dve.wait_ge(bt_done, 1)
                    v.tensor_copy(bv[:, :], bank[6][0:NG * BH, 0:DIST]).then_inc(bt_copied, 1)
                    dve.wait_ge(gtt_done, 1)
                    for j in range(2):
                        v.tensor_scalar(gz[:, j, :], bank[4][0:AH, j * S:(j + 1) * S],
                                        bif[:, j:j + 1], None, ALU.add).then_inc(gseq, 1)
                    dve.wait_ge(gact, 3)
                    v.tensor_tensor_scan(gn[:, :], gones[:, :], gl[:, :], 0.0, ALU.mult, ALU.add)\
                        .then_inc(gseq, 1)
                    dve.wait_ge(gseq, 3)
                    v.scalar_tensor_tensor(gc[:, :], gt[:, 0, :], CAP, gn[:, :], ALU.mult, ALU.add)\
                        .then_inc(gseq, 1)
                    dve.wait_ge(gseq, 4)
                    v.tensor_tensor_scan(gm[:, :], gc[:, :], gc[:, :], 0.0, ALU.max, ALU.max)\
                        .then_inc(gseq, 1)
                    dve.wait_ge(gseq, 5)
                    v.tensor_tensor(gd[:, :], gn[:, :], gm[:, :], ALU.subtract).then_inc(gseq, 1)
                if u == 5:
                    dve.wait_ge(ct_done, 1)
                    v.tensor_copy(cS[:, :, :].rearrange("p s h -> p (s h)"),
                                  bank[4][:, 0:NT * AH]).then_inc(cs_done, 1)
                    dve.wait_ge(cs_done, 1)
                    for h in range(AH):
                        dve.wait_ge(mb_done, 2 * (h // 2) + 2)
                        m = bank[5 + h // 2][:, (h % 2) * S:(h % 2 + 1) * S]
                        v.tensor_scalar(EE[:, h, 0:S], m, cS[:, 0, h:h + 1], 0.0,
                                        ALU.subtract, ALU.max).then_inc(ee_done, 1)
                        v.tensor_scalar(EE[:, h, S:384], m[:, P:S], cS[:, 1, h:h + 1], 0.0,
                                        ALU.subtract, ALU.max).then_inc(ee_done, 1)
                if u == 6:
                    for h in range(AH):
                        dve.wait_ge(s_done, h + 1)
                        dve.wait_ge(dm_done, 2)
                        v.scalar_tensor_tensor(SD[:, h, :], bank[3 + h][:, 0:384], DK ** -0.5,
                                               EE[:, h, :], ALU.mult, ALU.mult)\
                            .then_inc(sd_done, 1)
                for h in {7: (0, 1), 8: (2,), 9: (3,)}.get(u, ()):
                    dve.wait_ge(den_abs, h + 1)
                    v.tensor_tensor(den[:, h, :], den[:, h, :], EB[:, h, :], ALU.max)\
                        .then_inc(dmax_done, 1)
                    dve.wait_ge(dmax_done, h + 1)
                    v.reciprocal(dinv[:, h, :], den[:, h, :]).then_inc(dinv_done, 1)
                    dve.wait_ge(dinv_done, h + 1)
                    dve.wait_ge(num_done, h + 1)
                    v.tensor_tensor(hm[:, h, :, :],
                                    bank[3 + h][:, :].rearrange("p (c t) -> p c t", c=2),
                                    dinv[:, h:h + 1, :].to_broadcast([P, 2, S]), ALU.mult)\
                        .then_inc(hm_done, 1)
                if u in (8, 10):
                    b = u // 10
                    dve.wait_ge(hroot_done, b + 1)
                    v.reciprocal(hrs[:, 2 * b:2 * b + 2, :], hroot[:, 2 * b:2 * b + 2, :])\
                        .then_inc(hrs_done, 1)
                    dve.wait_ge(hrs_done, b + 1)
                    for h in (2 * b, 2 * b + 1):
                        v.tensor_tensor(hm[:, h, :, :], hm[:, h, :, :],
                                        hrs[:, h:h + 1, :].to_broadcast([P, 2, S]), ALU.mult)\
                            .then_inc(hn_done, 1)
                if u == 11:
                    for k in range(4):
                        gated(k)
                for c in range(2):
                    t = 2 * u + c
                    complete(c, T_IN + u, U_IN + u)
                    ps = bank[t % 3][:, 0:S]
                    if u < 2:
                        o = v.tensor_tensor(qT[:, 2 * u + c, :], ps, rstd[:, 0:S], ALU.mult)
                    elif u < 4:
                        o = v.tensor_tensor(kT[:, 2 * (u - 2) + c, :], ps, rstd[:, 0:S], ALU.mult)
                    elif u < 8:
                        o = v.tensor_scalar(Vm[:, c, (u - 4) * CW:(u - 3) * CW], ps,
                                            rstd[:, S + c:S + c + 1], None, ALU.mult)
                    else:
                        o = v.tensor_tensor(sig[:, 2 * (u - 8) + c, :], ps, rstd[:, 0:S], ALU.mult)
                    o.then_inc(ev_done, 1)
            for k in range(4, KD):
                gated(k)
                m_lo(k - 4)
            for k in range(4, KD):
                m_lo(k)

            def outproj(u0, t0, q0, x0, sets):
                acc_clear(q0)
                for u in range(4):
                    lo(u0 + u + 2)
                    for c in range(2):
                        residual(2 * u + c, c, t0 + u, u0 + u, c)
                    for c in range(2):
                        dve.wait_ge(x_new, q0 + 2 * u + c + 1 - KD)
                        post(2 * u + c, q0 + 2 * u + c, x0 + 2 * u + c, sets)

            outproj(U_AOUT, T_AOUT, 8, 8, ((xsA, V_F0),))

            def ffn(layer, u_up, t_up, u_down, t_down, q0, x0, sets, s):
                f0, p0 = 4 * PAIRS * layer, PAIRS * layer
                def read_out(p, g, n, i, step):
                    for c in range(2):
                        j = 2 * g + c
                        complete(c, p * 2 + (t_up + g), n + g, i, step)
                        ge(dve, cB_done, 4 * p + (f0 - 4 + j + 1))
                        v.tensor_tensor(ub[:, j, 2:S + 2], bank[FB[j]][:, 0:S], rstd[:, 0:S], ALU.mult)\
                            .then_inc(ev_done, 1)

                def taps(p, g):
                    for c in range(2):
                        j = 2 * g + c
                        dve.wait_ge(t1_done, 4 * p + (f0 + j + 1))
                        v.scalar_tensor_tensor(cb[:, j, :], ub[:, j, 1:S + 1],
                                               conv_col(layer, 1, p * 2 + (KF * g + c)),
                                               cb[:, j, :], ALU.mult, ALU.add).then_inc(cA_done, 1)
                    for c in range(2):
                        j = 2 * g + c
                        dve.wait_ge(cA_done, 4 * p + (f0 + j + 1))
                        v.scalar_tensor_tensor(cb[:, j, :], ub[:, j, 0:S],
                                               conv_col(layer, 0, p * 2 + (KF * g + c)),
                                               cb[:, j, :], ALU.mult, ALU.add).then_inc(cB_done, 1)

                def product(p):
                    dve.wait_ge(silu_done, p + (p0 + 1))
                    dve.wait_ge(cB_done, 4 * p + (f0 + 4))
                    v.tensor_tensor(hb_[:, :, :], gb[:, :, :], cb[:, 2:4, :], ALU.mult)\
                        .then_inc(mul_done, 1)

                def h_lo(p):
                    dve.wait_ge(hhi_done, p + (p0 + 1))
                    v.tensor_tensor(hs[:, bass.ds(2 * p, 2), 1, :], hb_[:, :, :],
                                    hs[:, bass.ds(2 * p, 2), 0, :].bitcast(F32), ALU.subtract)\
                        .then_inc(hlo_done, 1)

                def pair(n, p, i, step, first):
                    lo(n + 2, i, step)
                    if first:
                        rstd_of(s, S)
                    read_out(p, 0, n, i, step)
                    if not first:
                        taps(p - 1, 1)
                        product(p - 1)
                    lo(n + 3, i, step)
                    read_out(p, 1, n, i, step)
                    taps(p, 0)
                    if not first:
                        h_lo(p - 1)

                v.memset(ub[:, :, 0:2], 0.0).then_inc(pad_done, 1)
                dve.wait_ge(pad_done, layer + 1)
                pair(u_up, 0, 0, 0, True)
                with dve.Fori(0, 3) as i:
                    for j in range(3):
                        pair(u_up + 2 + 2 * j, i * 3 + (1 + j), i, 6, False)
                pair(u_up + 20, PAIRS - 1, 0, 0, False)
                taps(PAIRS - 1, 1)
                product(PAIRS - 1)
                h_lo(PAIRS - 1)
                acc_clear(q0)

                def column(i, n, ii, step, last):
                    lo(n + 2, ii, step)
                    lo(n + 3, ii, step)
                    lo(n + 4, ii, step)
                    m = 6 if last else 0
                    for c in range(2):
                        residual(i * 2 + c, c, i + t_down, n + 2, 4 + c, ii, step)
                    for c in range(2):
                        dve.wait_ge(x_new, q0 + m + c + 1 - KD + ii * (0 if last else 2))
                        post(i * 2 + c, q0 + m + c, x0 + (m + c) * len(sets), sets, ii,
                             0 if last else 2)

                with dve.Fori(0, 3) as i:
                    column(i, u_down, i, 3, False)
                column(3, u_down + 9, 0, 0, True)

            ffn(0, U_UP0, T_UP0, U_DOWN0, T_DOWN0, 16, 16, ((xsA, V_KV), (xsB, V_B)), 1)

            def block(i, step, last):
                n0 = U_BODY + (27 if last else 0)
                hb = NHB - 1 if last else i

                def evac(j, c):
                    read_qkv(n0 + j, i, step, hb * 9 + (2 + j), 2 + j, c, *BODY[j])

                def biased(s):
                    h, tt = divmod(s, 2)
                    w = P * (1 + tt)
                    dve.wait_ge(sc_done, hb * 8 + (s + 1))
                    if tt == 0:
                        dve.wait_ge(bi_in[h], hb * 16 + 16)
                    if s >= 2:
                        dve.wait_ge(tr_done, hb * 8 + (s - 1))
                    v.memset(carry[:, s % 2:s % 2 + 1], 0.0)
                    bb = Bi[:, h, :, :] if tt else Bi[:, h, :, P:S]
                    v.tensor_tensor_reduce(
                        out=SB[:, s % 2, 0:NG * w].rearrange("p (g f) -> p g f", g=NG),
                        in0=two[0][:, 0:NG * w].rearrange("p (g f) -> p g f", g=NG), in1=bb,
                        scale=1.0, scalar=-3e38, op0=ALU.add, op1=ALU.max,
                        accum_out=mxx[:, s:s + 1]).then_inc(smax_done, 1)
                    dve.wait_ge(smax_done, hb * 8 + (s + 1))
                    v.tensor_scalar(nmx[:, s:s + 1], mxx[:, s:s + 1], -1.0, None, ALU.mult)\
                        .then_inc(nmx_done, 1)

                def pt_copy(s):
                    h, tt = divmod(s, 2)
                    w = NG * (1 + tt)
                    dve.wait_ge(tr_done, hb * 8 + (s + 1))
                    v.tensor_copy(PT[:, h, 3 * tt:3 * tt + w, :].rearrange("p b q -> p (b q)"),
                                  two[1][:, 0:w * P]).then_inc(pt_done, 1)

                def normed(h):
                    dve.wait_ge(exp_done, hb * 8 + (2 * h + 2))
                    v.reciprocal(linv[:, 2 * h:2 * h + 2], lsum[:, 2 * h:2 * h + 2])\
                        .then_inc(linv_done, 1)
                    dve.wait_ge(linv_done, hb * HB + (h + 1))
                    dve.wait_ge(pv_done, hb * HB + (h + 1))
                    for tt in range(NT):
                        v.tensor_scalar(ohb[:, tt, h * DH:(h + 1) * DH],
                                        bank[(7, 4)[h % 2]][:, tt * DH:(tt + 1) * DH],
                                        linv[:, 2 * h + tt:2 * h + tt + 1], None, ALU.mult)\
                            .then_inc(o_done, 1)

                def a_lo(c):
                    dve.wait_ge(ahi_done, hb * 2 + (c + 1))
                    v.tensor_tensor(aTs[:, bass.ds(hb * 2 + c, 1), 1, :],
                                    bank[3][:, 0:S].rearrange("p (a t) -> p a t", a=1),
                                    aTs[:, bass.ds(hb * 2 + c, 1), 0, :].bitcast(F32), ALU.subtract)\
                        .then_inc(alo_done, 1)

                for j in range(4):
                    lo(n0 + j + 2, i, step)
                    evac(j, 0)
                    evac(j, 1)
                biased(0)
                for m in range(6):
                    if m % 2 == 0:
                        lo(n0 + 4 + m // 2 + 2, i, step)
                    evac(4 + m // 2, m % 2)
                    biased(m + 1)
                    pt_copy(m)
                if not last:
                    lo(n0 + 7 + 2, i, step)
                biased(7)
                pt_copy(6)
                if not last:
                    evac(7, 0)
                    evac(7, 1)
                normed(0)
                normed(1)
                pt_copy(7)
                if not last:
                    lo(n0 + 8 + 2, i, step)
                    evac(8, 0)
                normed(2)
                normed(3)
                a_lo(0)
                if not last:
                    evac(8, 1)
                a_lo(1)

            def read_qkv(n, i, step, m, u, c, kind, g):
                complete(c, m + T_QKV, n, i, step)
                ps = bank[(2 * u + c) % 3][:, 0:S]
                if kind == "q":
                    o = v.scalar_tensor_tensor(
                        QT[:, g, c, :].rearrange("p (a t) -> p a t", a=NT)[:, :, ::-1],
                        ps.rearrange("p (a t) -> p a t", a=NT), DH ** -0.5,
                        rstd[:, 0:S].rearrange("p (a t) -> p a t", a=NT), ALU.mult, ALU.mult)
                elif kind == "k":
                    o = v.tensor_tensor(KT[:, g, c, :], ps, rstd[:, 0:S], ALU.mult)
                else:
                    o = v.tensor_scalar(Va[:, c, g, :], ps, rstd[:, S + c:S + c + 1], None, ALU.mult)
                o.then_inc(ev_done, 1)

            lo(U_QKV + 2)
            rstd_of(2, S + NT)
            for u in range(2):
                if u:
                    lo(U_QKV + u + 2)
                for c in range(2):
                    read_qkv(U_QKV + u, 0, 0, u, u, c, "qk"[u], 0)
            with dve.Fori(0, NHB - 1) as i:
                block(i, 9, False)
            block(0, 0, True)
            outproj(U_BOUT, T_BOUT, 24, 32, ((xsB, V_F1),))
            ffn(1, U_UP1, T_UP1, U_DOWN1, T_DOWN1, 32, 40, (), 3)

            rstd_of(4, S)
            for k in range(KD):
                v.scalar_tensor_tensor(Y[:, k, :], X[:, k, :], col(V_FIN + k), rstd[:, 0:S],
                                       ALU.mult, ALU.mult).then_inc(yn_done, 1)

        @block.tensor
        def _(pe):
            t_ = nc.tensor

            def three(ps, hi_w, lo_w, hi_x, lo_x, first, last):
                t_.matmul(ps, hi_w, hi_x, start=first, stop=False)
                t_.matmul(ps, hi_w, lo_x, start=False, stop=False)
                return t_.matmul(ps, lo_w, hi_x, start=False, stop=last)

            def unit(n, xs, banks, i=0, step=0, ks=(0, KD), ktot=KD, wait_bank=(), k_wait=None,
                     token_major=False):
                s = n % RING
                pe.wait_ge(lo_done[s], rnd(n, i, step) + 1)
                k0, k1 = ks
                order = [(k, c) for k in range(k0, k1) for c in range(2)] if k_wait else \
                    [(k, c) for c in range(2) for k in range(k0, k1)]
                for k, c in order:
                    if k_wait and c == 0:
                        k_wait(k)
                    if k == k0 and c < len(wait_bank) and wait_bank[c] is not None:
                        ge(pe, *wait_bank[c])
                    cs = slice(c * P, (c + 1) * P)
                    first, last = k == 0, k == ktot - 1
                    kk = k - k0
                    if token_major:
                        ps = bank[banks[c]][:, 0:CW]
                        t_.matmul(ps, xs[:, k, 0, cs], whi[s][:, kk, :], start=first, stop=False)
                        t_.matmul(ps, xs[:, k, 0, cs], wlo[s][:, kk, :], start=False, stop=False)
                        mm = t_.matmul(ps, xs[:, k, 1, cs], whi[s][:, kk, :], start=False,
                                       stop=last)
                    else:
                        mm = three(bank[banks[c]][:, 0:S], whi[s][:, kk, cs], wlo[s][:, kk, cs],
                                   xs[:, k, 0, :], xs[:, k, 1, :], first, last)
                    if (k, c) == order[-1]:
                        mm.then_inc(w_used[s], 1)
                    elif last:
                        mm.then_inc(tile_done, 1)

            def sums(s, b, tokens):
                pe.wait_ge(acc_done, 8 * (s + 1))
                mm = t_.matmul(bank[b][:, 0:S], ones[:], acc[:, :], start=True, stop=True)
                if tokens:
                    for tt in range(NT):
                        mm = t_.matmul(bank[b][:, S + tt:S + tt + 1], acc[:, tt * P:(tt + 1) * P],
                                       ones[:, 0:1], start=True, stop=True)
                mm.then_inc(ss_done, 1)

            pe.wait_ge(consts, 10)
            for u in range(12):
                t = 2 * u
                waits = [(ev_done, t + c - 2) for c in range(2)]
                unit(U_IN + u, xsA, [t % 3, (t + 1) % 3], wait_bank=waits,
                     k_wait=(lambda k: pe.wait_ge(xlo_done, k + 1)) if u == 0 else None,
                     token_major=4 <= u < 8)
                if u == 0:
                    sums(0, 7, True)
                if u == 1:
                    pe.wait_ge(wgl_done, 1)
                    for tt in range(NT):
                        ps = bank[3][:, tt * 2 * AH:(tt + 1) * 2 * AH]
                        ts_ = slice(tt * P, (tt + 1) * P)
                        for k in range(KD):
                            t_.matmul(ps, xsA[:, k, 0, ts_], wgh[:, k, :], start=k == 0, stop=False)
                            t_.matmul(ps, xsA[:, k, 0, ts_], wgl[:, k, :], start=False, stop=False)
                            mm = t_.matmul(ps, xsA[:, k, 1, ts_], wgh[:, k, :], start=False,
                                           stop=k == KD - 1)
                    mm.then_inc(gates_ps, 1)
                if u == 2:
                    pe.wait_ge(c_in, 64)
                    t_.matmul(bank[6][0:NG * BH, 0:DIST], rb[:, :], oh[:, :], start=True,
                              stop=False)
                    t_.matmul(bank[6][0:NG * BH, 0:DIST], gs[:, :], mk[:, :], start=False,
                              stop=True).then_inc(bt_done, 1)
                    pe.wait_ge(gtm_done, 2)
                    for j in range(2):
                        for tt in range(NT):
                            mm = t_.transpose(bank[4][0:AH, j * S + tt * P:j * S + (tt + 1) * P],
                                              gtm[:, tt, j * AH:(j + 1) * AH], ident[:])
                    mm.then_inc(gtt_done, 1)
                if u == 4:
                    pe.wait_ge(gates_done, 1)
                    for st in range(NT):
                        mm = t_.transpose(bank[4][:, st * AH:(st + 1) * AH],
                                          gc[:, st * P:(st + 1) * P], ident[0:AH, 0:AH])
                    mm.then_inc(ct_done, 1)
                    for h in range(AH):
                        t_.matmul(bank[5 + h // 2][:, (h % 2) * S:(h % 2 + 1) * S], sel[:, h, :],
                                  gm[:, :], start=True, stop=True).then_inc(mb_done, 1)
                    for h in range(AH):
                        mm = t_.matmul(bank[(3, 7)[h // 2]][:, (h % 2) * S:(h % 2 + 1) * S],
                                       sel[:, h, :], gx[:, :], start=True, stop=True)
                        if h % 2:
                            mm.then_inc(eb_done, 1)
                if u == 5:
                    pe.wait_ge(ev_done, 8)
                    pe.wait_ge(ee_done, 2 * AH)
                    pe.wait_ge(eb_copied, 2)
                    for h in range(AH):
                        b = bank[3 + h]
                        t_.matmul(b[:, 0:S], kT[:, h, 0:P], qT[:, h, :], start=True, stop=True)
                        t_.matmul(b[:, S:384], kT[:, h, P:S], qT[:, h, P:S], start=True, stop=True)\
                            .then_inc(s_done, 1)
                for h in {6: (0, 1), 7: (2,), 8: (3,)}.get(u, ()):
                    b = bank[3 + h]
                    pe.wait_ge(ev_done, 2 * (4 + h) + 2)
                    pe.wait_ge(sd_done, h + 1)
                    ge(pe, den_abs, h)
                    t_.matmul(bank[7][:, 0:S], ones[:], SD[:, h, 0:S], start=True, stop=False)
                    t_.matmul(bank[7][:, P:S], ones[:], SD[:, h, S:384], start=False, stop=True)\
                        .then_inc(den_done, 1)
                    for c in range(2):
                        cs = slice(h * DV + c * P, h * DV + (c + 1) * P)
                        t_.matmul(b[:, c * S:(c + 1) * S], Vm[:, 0, cs], SD[:, h, 0:S],
                                  start=True, stop=False)
                        mm = t_.matmul(b[:, c * S + P:(c + 1) * S], Vm[:, 1, cs],
                                       SD[:, h, S:384], start=False, stop=True)
                    mm.then_inc(num_done, 1)
                if u in (7, 9):
                    for h in (0, 1) if u == 7 else (2, 3):
                        pe.wait_ge(hsq_done, h + 1)
                        ps = bank[3 + h // 2][:, (h % 2) * S:(h % 2 + 1) * S]
                        t_.matmul(ps, ones[:], hsq[:, h, 0, :], start=True, stop=False)
                        mm = t_.matmul(ps, ones[:], hsq[:, h, 1, :], start=False, stop=True)
                        if h % 2:
                            mm.then_inc(hss_done, 1)

            def outproj(u0, e0, xs, k_wait, q0):
                pe.wait_ge(ev_done, e0)
                for u in range(4):
                    unit(u0 + u, xs, [0, 1],
                         wait_bank=[(x_new, q0 - KD + 2 * u + c - 1) for c in range(2)] if u else (),
                         k_wait=None if u else k_wait)

            def ffn(u_up, e_up, u_down, p0, xs, x0, q0, s):
                def pair(n, p, i, step, first):
                    for g in range(2):
                        if first:
                            waits = [(x_new, q0 - KD - 1 + c) for c in range(2)] if g else ()
                        else:
                            waits = [(ev_done, 4 * p + (e_up - 4 + 2 * g + c + 1)) for c in range(2)]
                        unit(n + g, xs, FB[2 * g:2 * g + 2], i, step, wait_bank=waits,
                             k_wait=(lambda k: pe.wait_ge(xlo_done, x0 + k + 1))
                             if first and not g else None)
                        if first and not g:
                            sums(s, 6, False)

                pair(u_up, 0, 0, 0, True)
                with pe.Fori(0, 3) as i:
                    for j in range(3):
                        pair(u_up + 2 + 2 * j, i * 3 + (1 + j), i, 6, False)
                pair(u_up + 20, PAIRS - 1, 0, 0, False)
                with pe.Fori(0, 4) as i:
                    for j, ks in enumerate(DOWN_K):
                        pe.wait_ge(hlo_done, p0 + ks[1] // 2)
                        unit(u_down + j, hs, [4, 5], i, 3, ks, KF,
                             wait_bank=[(x_new, i * 2 + (q0 - KD + c - 1)) for c in range(2)]
                             if j == 0 else ())

            outproj(U_AOUT, E_UP0, xsB, lambda k: pe.wait_ge(mlo_done, k + 1), 8)
            ffn(U_UP0, E_UP0, U_DOWN0, 0, xsA, 8, 16, 1)

            def tile_of(n, i, step, ev, u, c, kind, k_wait=None):
                s = n % RING
                if c == 0:
                    pe.wait_ge(lo_done[s], rnd(n, i, step) + 1)
                pe.wait_ge(ev_done, ev + (c - 2))
                ps = bank[(2 * u + c) % 3][:, 0:CW]
                cs = slice(c * P, (c + 1) * P)
                xs = xsB if kind == "q" else xsA
                for k in range(KD):
                    if k_wait and c == 0:
                        k_wait(k)
                    first, last = k == 0, k == KD - 1
                    if kind == "v":
                        t_.matmul(ps, xs[:, k, 0, cs], whi[s][:, k, :], start=first, stop=False)
                        t_.matmul(ps, xs[:, k, 0, cs], wlo[s][:, k, :], start=False, stop=False)
                        mm = t_.matmul(ps, xs[:, k, 1, cs], whi[s][:, k, :], start=False, stop=last)
                    else:
                        mm = three(ps, whi[s][:, k, cs], wlo[s][:, k, cs], xs[:, k, 0, :],
                                   xs[:, k, 1, :], first, last)
                mm.then_inc(w_used[s] if c else tile_done, 1)

            def block(i, step, last):
                n0 = U_BODY + (27 if last else 0)
                hb = NHB - 1 if last else i

                def tile(j, c):
                    tile_of(n0 + j, i, step, hb * 18 + (E_QKV + 2 * (2 + j)), 2 + j, c, BODY[j][0])

                def scores(s):
                    h, tt = divmod(s, 2)
                    rows = slice((h % 2) * DH, (h % 2 + 1) * DH)
                    w = P * (1 + tt)
                    if s == 0:
                        pe.wait_ge(ev_done, hb * 18 + (E_QKV + 12))
                    else:
                        pe.wait_ge(smax_done, hb * 8 + s)
                    for g in range(NG):
                        mm = t_.matmul(two[0][:, g * w:(g + 1) * w],
                                       QT[rows, g, h // 2, tt * P:(tt + 1) * P],
                                       KT[rows, g, h // 2, 0:w], start=True, stop=True)
                    mm.then_inc(sc_done, 1)

                def turned(s):
                    tt = s % 2
                    pe.wait_ge(exp_done, hb * 8 + (s + 1))
                    if s:
                        pe.wait_ge(pt_done, hb * 8 + s)
                    for b in range(NG * (1 + tt)):
                        mm = t_.transpose(two[1][:, b * P:(b + 1) * P],
                                          SB[:, s % 2, b * P:(b + 1) * P], ident[:])
                    mm.then_inc(tr_done, 1)

                def mixed(h):
                    pe.wait_ge(pt_done, hb * 8 + (2 * h + 2))
                    if h == 0:
                        pe.wait_ge(ev_done, hb * 18 + (E_QKV + 18))
                    elif h == 1:
                        pe.wait_ge(smax_done, hb * 8 + 8)
                    else:
                        pe.wait_ge(o_done, hb * 8 + (2 * h - 2))
                    for tt in range(NT):
                        blocks = [(g, 0, g) for g in range(NG)] if tt == 0 else \
                            [(g, kt, 3 + 2 * g + kt) for g in range(NG) for kt in range(NT)]
                        for m, (g, kt, b) in enumerate(blocks):
                            mm = t_.matmul(bank[(7, 4)[h % 2]][:, tt * DH:(tt + 1) * DH],
                                           PT[:, h, b, :], Va[:, kt, g, h * DH:(h + 1) * DH],
                                           start=m == 0, stop=m == len(blocks) - 1)
                    mm.then_inc(pv_done, 1)

                def flipped(c):
                    pe.wait_ge(o_done, hb * 8 + (4 * c + 4))
                    if c:
                        pe.wait_ge(alo_done, hb * 2 + 1)
                    for tt in range(NT):
                        mm = t_.matmul(bank[3][:, tt * P:(tt + 1) * P],
                                       ohb[:, tt, c * P:(c + 1) * P], anti[:], start=True, stop=True)
                    mm.then_inc(flip_done, 1)

                for j in range(4):
                    tile(j, 0)
                    tile(j, 1)
                scores(0)
                for m in range(6):
                    tile(4 + m // 2, m % 2)
                    scores(m + 1)
                    turned(m)
                if not last:
                    tile(7, 0)
                scores(7)
                turned(6)
                if not last:
                    tile(7, 1)
                mixed(0)
                mixed(1)
                turned(7)
                if not last:
                    tile(8, 0)
                mixed(2)
                mixed(3)
                flipped(0)
                if not last:
                    tile(8, 1)
                flipped(1)

            for u in range(2):
                for c in range(2):
                    tile_of(U_QKV + u, 0, 0, E_QKV + 2 * u, u, c, "qk"[u],
                            (lambda k: pe.wait_ge(xlo_done, 16 + 2 * k + 2)) if u == 0 else None)
                if u == 0:
                    sums(2, 7, True)
            with pe.Fori(0, NHB - 1) as i:
                block(i, 9, False)
            block(0, 0, True)

            outproj(U_BOUT, E_UP1, aTs, lambda k: pe.wait_ge(alo_done, k + 1), 24)
            ffn(U_UP1, E_UP1, U_DOWN1, PAIRS, xsB, 32, 32, 3)
            sums(4, 6, False)


def laid_out(inputs):
    def cols(a):
        return np.asarray(a).reshape(-1, P).T

    g = {n: np.asarray(a) for n, a in inputs.items()}
    vectors = [g["a_norm_g"], g["kv_norm_g"], g["b_norm_g"], g["f_norm_g"][0], g["f_norm_g"][1],
               g["final_norm_g"], g["a_hnorm_g"]]
    for layer in range(2):
        vectors += [g["f_conv_w"][layer, j] for j in range(3)] + [g["f_conv_b"][layer]]
    arrays = {
        "xT": g["x"][0].reshape(S, KD, P).transpose(2, 1, 0),
        "vectors": np.concatenate([cols(v) for v in vectors], axis=1),
        "b_if": g["a_b_if"][0].reshape(2, AH).T,
    }
    for n in ("a_w_in", "a_w_out", "w_kv", "b_w_q", "b_w_out", "rel_bias", "f_w_up", "f_w_down"):
        arrays[n] = g[n]
    arrays.update(zip(("onehot", "mask", "group"), distance_tables()))
    return {n: np.ascontiguousarray(a) for n, a in arrays.items()}


def kernel(**inputs):
    import concourse.bacc as bacc
    from concourse.bass_utils import run_bass_kernel_spmd

    nc = bacc.Bacc("TRN2", target_bir_lowering=False, num_devices=1)
    arrays = laid_out(inputs)
    args = [nc.dram_tensor(f"in_{n}", a.shape, mybir.dt.from_np(a.dtype), kind="ExternalInput").ap()
            for n, a in arrays.items()]
    out = nc.dram_tensor("out", (P, KD, S), F32, kind="ExternalOutput").ap()
    build(nc, *args, out)
    r = run_bass_kernel_spmd(nc, [{f"in_{n}": a for n, a in arrays.items()}], core_ids=[0])
    return np.ascontiguousarray(r.results[0]["out"].transpose(2, 1, 0).reshape(1, S, D))
```

```python
from contextlib import ExitStack

import concourse.bass as bass
import numpy as np
from concourse import mybir

P = 128
D = 1024
S = 256
KD = D // P
NT = S // P
CW = 256
SLOT = KD * CW
RING = 3
AH, DK, DV = 4, 128, 256
FF = 2816
KF = FF // P
PAIRS = FF // CW
NG, BH, DH = 3, 16, 64
HB = CW // DH
NHB = BH // HB
EPS = 1e-6
CAP = 15.0
BUCKETS, MAXD = 32, 2048
GROUPS = ((128, 1), (512, 4), (2048, 16))
DIST = 384
MASKED = -1e30

DOWN_K = ((0, 8), (8, 16), (16, 22))
U_IN, U_AOUT = 0, 12
U_UP0, U_DOWN0 = 16, 38
U_QKV, U_BOUT = 50, 86
U_UP1, U_DOWN1 = 90, 112
U_END = 124
T_IN, T_AOUT = 0, 12
T_UP0, T_DOWN0 = 16, 38
T_QKV, T_BOUT = 42, 78
T_UP1, T_DOWN1 = 82, 104
E_UP0, E_QKV, E_UP1, E_END = 24, 68, 140, 184
SHARE = 5
OB0, OB1 = ((4, 5), (0, 1), (2, 3), (4, 5)), ((0, 1), (2, 3), (4, 5), (0, 1))
HEAD_K = 6
Y_POOL = 5
FB = (2, 3, 0, 1)
V_A, V_KV, V_B, V_F0, V_F1, V_FIN, V_HN = range(0, 56, 8)
V_CONV = 56
V_END = V_CONV + 2 * 4 * 2 * KF
BODY = (("q", 1), ("k", 1), ("q", 2), ("k", 2), ("v", 0), ("v", 1), ("v", 2), ("q", 0), ("k", 0))
U_BODY = 52

F32 = mybir.dt.float32
F32R = mybir.dt.float32r
ALU = mybir.AluOpType
ACT = mybir.ActivationFunctionType


def distance_tables():
    dist = 255 - np.arange(DIST)
    exact = BUCKETS // 2
    d = np.maximum(dist, 0)
    ratio = np.log(np.maximum(d, 1) / exact) / np.log(MAXD / exact)
    large = np.minimum(exact + (ratio * (BUCKETS - exact)).astype(np.int64), BUCKETS - 1)
    bucket = np.where(d < exact, d, large)
    onehot = (bucket[None, :] == np.arange(BUCKETS)[:, None]).astype(np.float32)
    mask = np.stack([np.where((dist >= 0) & (dist % dil == 0) & (dist <= win), 0.0, MASKED)
                     for win, dil in GROUPS]).astype(np.float32)
    group = np.repeat(np.eye(NG, dtype=np.float32), BH, axis=1)
    return onehot, mask, group


def build(nc, xT, vectors, b_if, a_w_in, a_w_out, w_kv, b_w_q, b_w_out, rel_bias, f_w_up,
          f_w_down, onehot, mask, group, out):
    ctx = ExitStack()
    with ctx:
        sems = {}

        def sem(name):
            sems[name] = ctx.enter_context(nc.semaphore(name))
            return sems[name]

        at = [(int(nc.sbuf_base) + 63) // 64 * 64]

        def place(name, shape, dt=F32, arena=None):
            cur = at if arena is None else arena
            n = 4
            for s in shape[1:]:
                n *= s
            t = nc.alloc_sbuf_tensor_at(name, shape, dt, offset=cur[0])
            cur[0] += (n + 63) // 64 * 64
            return t

        raw = [place(f"raw{s}", [P, SLOT]) for s in range(RING)]
        whi = [place(f"whi{s}", [P, KD, CW], F32R) for s in range(RING)]
        wlo = [place(f"wlo{s}", [P, KD, CW], F32R) for s in range(RING)]
        X = place("X", [P, KD, S])
        xsA = place("xsA", [P, KD, 2, S], F32R)
        xsB = place("xsB", [P, KD, 2, S], F32R)
        ident = place("ident", [P, P])
        ones = place("ones", [P, P])
        vcols = place("vcols", [P, V_END])
        acc = place("acc", [P, S])
        sq = place("sq", [P, 2, S])
        rstd = place("rstd", [P, S + NT])
        bif = place("bif", [AH, 2])
        epsc = place("epsc", [P, 1])
        onec = place("onec", [P, 1])
        wroot = place("wroot", [P, 1])
        base = at[0]

        ar = [base]
        hm = place("hm", [P, AH, 2, S], F32, ar)
        hsq = place("hsq", [P, AH, 2, S], F32, ar)
        wg = place("wg", [P, KD, 2 * AH], F32, ar)
        wg4 = place("wg4", [P, KD, 4, 32], F32R, ar)
        gtmp = place("gtmp", [64, S], F32, ar)
        qk_at = ar[0]
        qT = place("qT", [P, AH, S], F32, ar)
        kT = place("kT", [P, AH, S], F32, ar)
        Vm = place("Vm", [P, NT, AH * DV], F32, ar)
        sig = place("sig", [P, KD, S], F32, ar)
        gz = place("gz", [AH, 2, S], F32, ar)
        gt = place("gt", [AH, 2, S], F32, ar)
        gp = place("gp", [AH, S], F32, ar)
        gl = place("gl", [AH, S], F32, ar)
        gn = place("gn", [AH, S], F32, ar)
        gc = place("gc", [AH, S], F32, ar)
        gm = place("gm", [AH, S], F32, ar)
        gd = place("gd", [AH, S], F32, ar)
        gx = place("gx", [AH, S], F32, ar)
        gones = place("gones", [AH, S], F32, ar)
        sel = place("sel", [64, AH, P], F32, ar)
        selr = place("selr", [64, AH, P], F32R, ar)
        gmx = place("gmx", [64, 2, S], F32R, ar)
        bv = place("bv", [NG * BH, DIST], F32, ar)
        oh = place("oh", [BUCKETS, DIST], F32, ar)
        mk = place("mk", [NG, DIST], F32, ar)
        gs = place("gs", [NG, NG * BH], F32, ar)
        rb = place("rb", [BUCKETS, NG * BH], F32, ar)
        cS = place("cS", [P, NT, AH], F32, ar)
        EE = place("EE", [P, AH, 384], F32, ar)
        SD = place("SD", [P, AH, 384], F32, ar)
        EB = place("EB", [P, AH, S], F32, ar)
        den = place("den", [P, AH, S], F32, ar)
        assert ar[0] <= nc.sbuf_usable_end, ar[0]
        hroot = place("hroot", [P, AH, S], F32, [qk_at])
        hrs = place("hrs", [P, AH, S], F32, [qk_at + AH * S * 4])

        ar = [base]
        hs = place("hs", [P, KF, 2, S], F32R, ar)
        ub = place("ub", [P, 4, S + 2], F32, ar)
        cb = place("cb", [P, 4, S], F32, ar)
        gb = place("gb", [P, 2, S], F32, ar)
        hb_ = place("hb", [P, 2, S], F32, ar)
        ar = [base]
        QT = place("QT", [P, NG, 2, S], F32, ar)
        KT = place("KT", [P, NG, 2, S], F32, ar)
        Vh = place("Vh", [P, NT, NG, CW], F32R, ar)
        Vl = place("Vl", [P, NT, NG, CW], F32R, ar)
        PTh = place("PTh", [P, HB, NG, 3, P], F32R, ar)
        PTl = place("PTl", [P, HB, NG, 3, P], F32R, ar)
        Bi = place("Bi", [P, 2, NG, S], F32, ar)
        SB = place("SB", [P, 2, NG * S], F32, ar)
        aTs = place("aTs", [P, KD, 2, S], F32R, ar)
        nmx = place("nmx", [P, 2 * HB], F32, ar)
        mxx = place("mxx", [P, 2 * HB], F32, ar)
        lsum = place("lsum", [P, 2 * HB], F32, ar)
        linv = place("linv", [P, 2 * HB], F32, ar)
        carry = place("carry", [P, 2], F32, ar)
        assert ar[0] <= nc.sbuf_usable_end, ar[0]
        ar = [base]
        Y = place("Y", [P, KD, S], F32, ar)
        assert at[0] <= nc.sbuf_usable_end

        bank = [ctx.enter_context(nc.psum_tensor(f"bank{b}", [P, 512], F32)) for b in range(3)]
        two = [ctx.enter_context(nc.psum_tensor(f"banks{b}", [P, 1024], F32)) for b in (34, 56)]
        bank += [two[0][:, 0:512], two[0][:, 512:1024], two[1][:, 0:512], two[1][:, 512:1024]]
        bank.append(ctx.enter_context(nc.psum_tensor("bank7", [P, 512], F32)))

        bvd = nc.dram_tensor("bias_by_distance", (NG * BH, DIST), F32, kind="Internal")

        raw_in = [sem(f"raw_in{s}") for s in range(RING)]
        hi_done = [sem(f"hi_done{s}") for s in range(RING)]
        lo_done = [sem(f"lo_done{s}") for s in range(RING)]
        w_used = [sem(f"w_used{s}") for s in range(RING)]
        x_in = [sem("x_in0"), sem("x_in1")]
        first_in, first_hi, first_lo = sem("first_in"), sem("first_hi"), sem("first_lo")
        share_lo = sem("share_lo")
        v_in, c_in, g_in = sem("v_in"), sem("c_in"), sem("g_in")
        bv_out, bi_in, y_out = sem("bv_out"), [sem(f"bi_in{h}") for h in range(HB)], sem("y_out")
        consts = sem("consts")
        bt_done, bt_copied = sem("bt_done"), sem("bt_copied")
        tile_done = sem("tile_done")
        ev_done = sem("ev_done")
        x_new = sem("x_new")
        sq_done = sem("sq_done")
        acc_zero = sem("acc_zero")
        acc_done = sem("acc_done")
        xhi_done = sem("xhi_done")
        xlo_done = sem("xlo_done")
        warm = sem("warm")
        ss_done = sem("ss_done")
        root_done, rstd_done = sem("root_done"), sem("rstd_done")
        wgh_done, wgl_done, gtmp_done = sem("wgh_done"), sem("wgl_done"), sem("gtmp_done")
        gates_ps, gseq, gact = sem("gates_ps"), sem("gseq"), sem("gact")
        gates_done, gmx_hi, gmx_lo = sem("gates_done"), sem("gmx_hi"), sem("gmx_lo")
        ct_done, mb_done, eb_done = sem("ct_done"), sem("mb_done"), sem("eb_done")
        cs_done, eb_copied = sem("cs_done"), sem("eb_copied")
        ee_done, dm_exp, dm_done = sem("ee_done"), sem("dm_exp"), sem("dm_done")
        s_done, sd_done = sem("s_done"), sem("sd_done")
        den_done, den_abs, dmax_done, dinv_done = (sem("den_done"), sem("den_abs"),
                                                   sem("dmax_done"), sem("dinv_done"))
        num_done, hm_done, hsq_done = sem("num_done"), sem("hm_done"), sem("hsq_done")
        hss_done, hroot_done, hrs_done = sem("hss_done"), sem("hroot_done"), sem("hrs_done")
        sig_done, hn_done, hg_done = sem("sig_done"), sem("hn_done"), sem("hg_done")
        mhi_done, mlo_done = sem("mhi_done"), sem("mlo_done")
        pad_done = sem("pad_done")
        t1_done, cA_done, cB_done = sem("t1_done"), sem("cA_done"), sem("cB_done")
        silu_done, mul_done = sem("silu_done"), sem("mul_done")
        hhi_done, hlo_done = sem("hhi_done"), sem("hlo_done")
        sc_done, smax_done, nmx_done = sem("sc_done"), sem("smax_done"), sem("nmx_done")
        exp_done, linv_done, p_done = sem("exp_done"), sem("linv_done"), sem("p_done")
        tr_done, pthi_done, ptlo_done = sem("tr_done"), sem("pthi_done"), sem("ptlo_done")
        vhi_done, pv_done = sem("vhi_done"), sem("pv_done")
        ahi_done, alo_done = sem("ahi_done"), sem("alo_done")
        yg_done = sem("yg_done")
        yn_done, yp_done = sem("yn_done"), sem("yp_done")

        block = ctx.enter_context(nc.Block())

        def rnd(n, i=0, step=0):
            return n // RING + i * (step // RING) if step else n // RING

        def ge(eng, s, v):
            if not (isinstance(v, int) and v <= 0):
                eng.wait_ge(s, v)

        def col(c):
            return vcols[:, c:c + 1]

        def head_out(hb, h, part):
            rows = slice((h % 2) * DH, (h % 2 + 1) * DH)
            dst = aTs[rows, bass.ds(hb * 2 + h // 2, 1), part, :]\
                .rearrange("p a (b t) -> p (a b) t", b=NT)
            src = bank[(7, 4)[h // 2]][rows, (h % 2) * S:(h % 2 + 1) * S]\
                .rearrange("p (b t) -> p b t", b=NT)[:, :, ::-1]
            return dst, src

        def n_v(n):
            last, j = divmod(n - U_BODY, 27)
            return last * 18 + 2 * (j - 4)

        def in_bank(t):
            return 5 if t == 3 else t % 3

        def qkv_bank(u, c, prologue):
            return 5 if prologue and 2 * u + c == 3 else (2 * u + c) % 3

        def conv_col(layer, tap, ch):
            return vcols[:, bass.ds(ch + (V_CONV + (4 * layer + tap) * 2 * KF), 1)]

        @block.sync
        def _(sp):
            def load(n, i, step, src, nk):
                s = n % RING
                if n >= RING:
                    sp.wait_ge(lo_done[s], rnd(n, i, step))
                sp.dma_start(raw[s][:, 0:nk * CW].rearrange("p (k c) -> p k c", c=CW),
                             src).then_inc(raw_in[s], 16)

            def cols(w, c):
                return w.rearrange("(k p) n -> p k n", p=P)[:, :, bass.ds(c, CW)]

            w_in = a_w_in[0]
            for half in range(2):
                ks = slice(4 * half, 4 * half + 4)
                sp.dma_start(X[:, ks, :], xT[:, ks, :]).then_inc(x_in[half], 16)
                sp.dma_start(raw[0][:, half * SLOT // 2:(half + 1) * SLOT // 2]
                             .rearrange("p (k c) -> p k c", c=CW), cols(w_in, 0)[:, ks, :])\
                    .then_inc(raw_in[0] if half else first_in, 16)
            for u in range(1, 12):
                if u == 4:
                    sp.wait_ge(share_lo, 1)
                load(U_IN + u, 0, 0, cols(w_in, u * CW), KD)
            for u in range(4):
                load(U_AOUT + u, 0, 0, cols(a_w_out[0], u * CW), KD)

            def ffn(layer, u_up, u_down):
                w = f_w_up[layer]

                def pair(n, i, step, p):
                    load(n, i, step, cols(w, p * CW), KD)
                    load(n + 1, i, step, cols(w, p * CW + FF), KD)

                pair(u_up, 0, 0, 0)
                with sp.Fori(0, 3) as i:
                    for j in range(3):
                        pair(u_up + 2 + 2 * j, i, 6, i * 3 + (1 + j))
                pair(u_up + 20, 0, 0, PAIRS - 1)
                wd = f_w_down[layer].rearrange("(k p) n -> p k n", p=P)
                with sp.Fori(0, 4) as i:
                    for j, (k0, k1) in enumerate(DOWN_K):
                        load(u_down + j, i, 3, wd[:, k0:k1, bass.ds(i * CW, CW)], k1 - k0)

            ffn(0, U_UP0, U_DOWN0)
            def block_unit(n, i, step, hb, kind, g):
                w = b_w_q[0] if kind == "q" else w_kv
                load(n, i, step, cols(w, hb * CW + (g + NG * (kind == "v")) * D), KD)

            block_unit(U_QKV, 0, 0, 0, "q", 0)
            block_unit(U_QKV + 1, 0, 0, 0, "k", 0)
            with sp.Fori(0, NHB - 1) as i:
                for j, (kind, g) in enumerate(BODY):
                    block_unit(U_BODY + j, i, 9, i + 1 if j >= 7 else i, kind, g)
            for j, (kind, g) in enumerate(BODY[:7]):
                block_unit(U_BODY + 27 + j, 0, 0, NHB - 1, kind, g)
            for u in range(4):
                load(U_BOUT + u, 0, 0, cols(b_w_out[0], u * CW), KD)
            ffn(1, U_UP1, U_DOWN1)
            for done, n, k0, k1 in ((yn_done, 2, 0, 2), (yn_done, Y_POOL, 2, Y_POOL),
                                    (yp_done, 2, Y_POOL, Y_POOL + 2),
                                    (yp_done, KD - Y_POOL, Y_POOL + 2, KD)):
                sp.wait_ge(done, n)
                sp.dma_start(out[:, k0:k1, :], Y[:, k0:k1, :]).then_inc(y_out, 16)
            sp.wait_ge(y_out, 16 * 4)
            sp.wait_ge(bv_out, 16)

        @block.gpsimd
        def _(pool):
            g = nc.gpsimd
            g.memset(epsc[:], EPS).then_inc(consts, 1)
            g.memset(wg4[:, :, :, :].bitcast(F32), 0.0).then_inc(consts, 1)
            g.memset(ident[:], 0.0).then_inc(consts, 1)
            g.memset(gmx[:, :, :].bitcast(F32), 0.0).then_inc(consts, 1)
            g.memset(sel[:], 0.0).then_inc(consts, 1)
            g.memset(ones[:], 1.0).then_inc(consts, 1)
            g.memset(onec[:], 1.0).then_inc(consts, 1)
            g.memset(gones[:], 1.0).then_inc(consts, 1)
            pool.wait_ge(consts, 8)
            g.affine_select(out=ident[:], in_=ident[:], compare_op=ALU.not_equal, fill=1.0, base=0,
                            pattern=[[-1, P]], channel_multiplier=1).then_inc(consts, 1)
            for base_ in (0, -32):
                g.affine_select(out=sel[:], in_=sel[:], compare_op=ALU.not_equal, fill=1.0,
                                base=base_, pattern=[[-1, AH], [0, P]], channel_multiplier=1)\
                    .then_inc(consts, 1)
                pool.wait_ge(consts, 10 if base_ == 0 else 11)
            g.tensor_copy(selr[:, :, :], sel[:, :, :]).then_inc(consts, 1)

            def lo(n, i=0, step=0, k0=0):
                s = n % RING
                pool.wait_ge(hi_done[s], rnd(n, i, step) + 1)
                g.tensor_tensor(wlo[s][:, k0:KD, :],
                                raw[s][:, k0 * CW:SLOT].rearrange("p (k c) -> p k c", c=CW),
                                whi[s][:, k0:KD, :].bitcast(F32), ALU.subtract)\
                    .then_inc(lo_done[s], 1)

            for n in range(U_IN, 6):
                if n % RING:
                    lo(n, k0=SHARE if n == 1 else 0)
            pool.wait_ge(dm_exp, 2 * AH)
            g.affine_select(out=EE[:, :, 0:S], in_=EE[:, :, 0:S], compare_op=ALU.is_ge, fill=0.0,
                            base=0, pattern=[[0, AH], [1, S]], channel_multiplier=-1)\
                .then_inc(dm_done, 1)
            g.affine_select(out=EE[:, :, S:384], in_=EE[:, :, S:384], compare_op=ALU.is_ge,
                            fill=0.0, base=0, pattern=[[0, AH], [1, P]], channel_multiplier=-1)\
                .then_inc(dm_done, 1)
            with pool.Fori(0, (U_END - 7) // RING) as i:
                for n in (7, 8):
                    lo(n, i, RING)
            pool.wait_ge(rstd_done, 5)
            for k in range(Y_POOL, KD):
                pool.wait_ge(yg_done, k - Y_POOL + 1)
                g.tensor_tensor(Y[:, k, :], Y[:, k, :], rstd[:, 0:S], ALU.mult)\
                    .then_inc(yp_done, 1)

        @block.scalar
        def _(act):
            a = nc.scalar

            def hi(n, i=0, step=0, k0=0, k1=KD):
                s = n % RING
                act.wait_ge(raw_in[s], (rnd(n, i, step) + 1) * 16)
                if n >= RING:
                    act.wait_ge(w_used[s], rnd(n, i, step))
                o = a.activation(whi[s][:, k0:k1, :], raw[s][:, k0 * CW:k1 * CW]
                                 .rearrange("p (k c) -> p k c", c=CW), ACT.Copy)
                if k1 == KD:
                    o.then_inc(hi_done[s], 1)

            def gained(k, sets):
                for dst, gain in sets:
                    a.activation(dst[:, bass.ds(k, 1), 0, :], X[:, bass.ds(k, 1), :], ACT.Copy,
                                 scale=vcols[:, bass.ds(k + gain, 1)]).then_inc(xhi_done, 1)

            def squared(k, q):
                a.activation(sq[:, q % 2, :], X[:, bass.ds(k, 1), :].rearrange("p a t -> p (a t)"),
                             ACT.Square).then_inc(sq_done, 1)

            def post(k, q, sets, i=0, dq=0):
                act.wait_ge(x_new, q + i * dq + (1 - KD))
                act.wait_ge(acc_done, q + i * dq - 1)
                gained(k, sets)
                squared(k, q)

            def warm_root():
                a.activation(wroot[:, :], epsc[:, :], ACT.Sqrt).then_inc(warm, 1)

            def root_of(s, width, b):
                act.wait_ge(ss_done, s + 1)
                if s:
                    act.wait_ge(rstd_done, s)
                a.activation(rstd[:, 0:width], bank[b][:, 0:width], ACT.Sqrt, bias=epsc[:, 0:1],
                             scale=1.0 / D).then_inc(root_done, 1)

            def gate(k):
                act.wait_ge(ev_done, 16 + k + 1)
                a.activation(sig[:, k, :], sig[:, k, :], ACT.Sigmoid).then_inc(sig_done, 1)

            def m_hi(k):
                act.wait_ge(hg_done, k + 1)
                a.activation(xsB[:, k, 0, :], hm[:, k // 2, k % 2, :], ACT.Copy)\
                    .then_inc(mhi_done, 1)

            act.dma_start(vcols[:, :], vectors).then_inc(v_in, 16)
            act.wait_ge(consts, 1)
            warm_root()
            act.wait_ge(v_in, 16)
            for half in range(2):
                act.wait_ge(x_in[half], 16)
                for k in range(4 * half, 4 * half + 4):
                    gained(k, ((xsA, V_A),))
                if half == 0:
                    act.wait_ge(first_in, 16)
                    a.activation(whi[0][:, 0:4, :], raw[0][:, 0:4 * CW]
                                 .rearrange("p (k c) -> p k c", c=CW), ACT.Copy)\
                        .then_inc(first_hi, 1)
            hi(0, k0=4)
            for k in range(4):
                ge(act, acc_done, k - 1)
                squared(k, k)
            act.dma_start(wg[:, :, :], a_w_in[0].rearrange("(k p) n -> p k n", p=P)
                          [:, :, 12 * CW:12 * CW + 2 * AH]).then_inc(g_in, 16)
            hi(1)
            for k in range(4, KD):
                act.wait_ge(acc_done, k - 1)
                squared(k, k)
            act.dma_start(bif[:, :], b_if).then_inc(g_in, 16)
            hi(2)
            root_of(0, S + NT, 7)
            act.wait_ge(g_in, 32)
            act.wait_ge(consts, 12)
            a.activation(wg4[:, :, 0:2, 0:AH], wg[:, :, :].rearrange("p k (j h) -> p k j h", j=2),
                         ACT.Copy).then_inc(wgh_done, 1)
            act.dma_start(oh[:], onehot).then_inc(c_in, 16)
            act.dma_start(mk[:], mask).then_inc(c_in, 16)
            act.dma_start(gs[:], group).then_inc(c_in, 16)
            act.dma_start(rb[:], rel_bias).then_inc(c_in, 16)
            for u in range(12):
                if u == 3:
                    act.wait_ge(gseq, 2)
                    a.activation(gt[:, :, :], gz[:, :, :], ACT.Tanh, scale=1.0 / CAP).then_inc(gact, 1)
                    act.wait_ge(gact, 1)
                    a.activation(gp[:, :], gt[:, 1, :], ACT.Exp, scale=-CAP).then_inc(gact, 1)
                    act.wait_ge(gact, 2)
                    a.activation(gl[:, :], gp[:, :], ACT.Ln, bias=onec[0:AH, 0:1])\
                        .then_inc(gact, 1)
                    act.wait_ge(bt_copied, 1)
                    act.dma_start(bvd.ap(), bv[:, :]).then_inc(bv_out, 16)
                    act.wait_ge(gseq, 6)
                    a.activation(gx[:, :], gd[:, :], ACT.Exp).then_inc(gates_done, 1)
                if u == 5:
                    for b in range(2):
                        act.wait_ge(eb_done, b + 1)
                        a.activation(EB[:, 2 * b:2 * b + 2, :],
                                     bank[(3, 7)[b]][:, :].rearrange("p (h t) -> p h t", h=2),
                                     ACT.Copy).then_inc(eb_copied, 1)
                    for e in range(2 * AH):
                        h, st = divmod(e, 2)
                        c = slice(0, S) if st == 0 else slice(S, 384)
                        act.wait_ge(ee_done, e + 1)
                        a.activation(EE[:, h, c], EE[:, h, c], ACT.Exp, scale=-1.0)\
                            .then_inc(dm_exp, 1)
                for h in {7: (0, 1), 8: (2,), 9: (3,)}.get(u, ()):
                    act.wait_ge(den_done, h + 1)
                    a.activation(den[:, h, :], bank[7][:, 0:S], ACT.Abs).then_inc(den_abs, 1)
                    act.wait_ge(hm_done, h + 1)
                    a.activation(hsq[:, h, :, :], hm[:, h, :, :], ACT.Square).then_inc(hsq_done, 1)
                if u in (8, 10):
                    b = u // 10
                    act.wait_ge(hss_done, b + 1)
                    a.activation(hroot[:, 2 * b:2 * b + 2, :],
                                 bank[3 + b][:, :].rearrange("p (h t) -> p h t", h=2),
                                 ACT.Sqrt, bias=epsc[:, 0:1], scale=1.0 / DV)\
                        .then_inc(hroot_done, 1)
                if u == 10:
                    for k in range(4):
                        gate(k)
                if u == 11:
                    for k in (4, 5):
                        gate(k)
                    for k in range(4):
                        m_hi(k)
                else:
                    hi(u + 3)
            for k in (6, 7):
                gate(k)
            for k in range(4, KD):
                m_hi(k)
            hi(14)
            def projected(u0, q0, sets):
                hi(u0 + 3)
                for u in range(4):
                    if u == 3:
                        for c in range(2):
                            act.wait_ge(x_new, q0 + 6 + c + (1 - KD))
                            gained(6 + c, sets)
                        for c in range(2):
                            act.wait_ge(acc_done, q0 + 6 + c - 1)
                            squared(6 + c, q0 + 6 + c)
                        warm_root()
                    else:
                        for c in range(2):
                            post(2 * u + c, q0 + 2 * u + c, sets)
                    for n in ((4,), (5,), (), (6,))[u]:
                        hi(u0 + n)

            projected(U_AOUT, 8, ((xsA, V_F0),))

            def ffn(layer, u_up, e_up, u_down, q0, sets, s):
                f0, p0 = 4 * PAIRS * layer, PAIRS * layer

                def first_tap(p, g):
                    for c in range(2):
                        j = 2 * g + c
                        act.wait_ge(ev_done, 4 * p + (e_up + j + 1))
                        ge(act, mul_done if g else silu_done, p + p0)
                        ch = p * 2 + (KF * g + c)
                        a.activation(cb[:, j, :], ub[:, j, 2:S + 2], ACT.Identity,
                                     scale=conv_col(layer, 2, ch), bias=conv_col(layer, 3, ch))\
                            .then_inc(t1_done, 1)

                def h_hi(p):
                    act.wait_ge(mul_done, p + (p0 + 1))
                    a.activation(hs[:, bass.ds(p * 2, 2), 0, :], hb_[:, :, :], ACT.Copy)\
                        .then_inc(hhi_done, 1)

                def pair(n, p, i, step, first):
                    if first:
                        root_of(s, S, 6)
                    hi(n + 3, i, step)
                    first_tap(p, 0)
                    if not first:
                        h_hi(p - 1)
                    hi(n + 4, i, step)
                    first_tap(p, 1)
                    act.wait_ge(cB_done, 4 * p + (f0 + 2))
                    ge(act, mul_done, p + p0)
                    a.activation(gb[:, :, :], cb[:, 0:2, :], ACT.Silu).then_inc(silu_done, 1)

                pair(u_up, 0, 0, 0, True)
                with act.Fori(0, 3) as i:
                    for j in range(3):
                        pair(u_up + 2 + 2 * j, i * 3 + (1 + j), i, 6, False)
                pair(u_up + 20, PAIRS - 1, 0, 0, False)
                h_hi(PAIRS - 1)
                with act.Fori(0, 3) as i:
                    hi(u_down + 3, i, 3)
                    hi(u_down + 4, i, 3)
                    for c in range(2):
                        post(i * 2 + c, q0 + c, sets, i, 2)
                    hi(u_down + 5, i, 3)
                for n in (12, 13):
                    if u_down + n < U_END:
                        hi(u_down + n)
                warm_root()
                for k in (6, 7):
                    post(k, q0 + k, sets)
                if u_down + 14 < U_END:
                    hi(u_down + 14)

            ffn(0, U_UP0, E_UP0, U_DOWN0, 16, ((xsA, V_KV), (xsB, V_B)), 1)

            def block(i, step, last):
                n0 = U_BODY + (27 if last else 0)
                hb = NHB - 1 if last else i
                def load_bias(h):
                    src = bass.AP(bvd, (hb * HB + h) * DIST, [[1, P], [BH * DIST, NG], [1, S]])
                    act.dma_start(Bi[:, h % 2, :, :], src).then_inc(bi_in[h], 16)

                def soft(s):
                    h, tt = divmod(s, 2)
                    w = NG * P * (1 + tt)
                    act.wait_ge(nmx_done, hb * 8 + (s + 1))
                    a.activation(SB[:, s % 2, 0:w], SB[:, s % 2, 0:w], ACT.Exp,
                                 bias=nmx[:, s:s + 1], accum_out=lsum[:, s:s + 1])\
                        .then_inc(exp_done, 1)

                def v_hi(j, c):
                    if c:
                        act.wait_ge(w_used[(n0 + j) % RING], rnd(n0 + j, i, step) + 1)
                    else:
                        act.wait_ge(tile_done, hb * 9 + (T_QKV + 2 + j + 1))
                    a.activation(Vh[:, c, BODY[j][1], :], bank[(2 * (2 + j) + c) % 3][:, 0:S],
                                 ACT.Copy, scale=rstd[:, S + c:S + c + 1]).then_inc(vhi_done, 1)

                def p_hi(s):
                    h, tt = divmod(s, 2)
                    act.wait_ge(tr_done, hb * 8 + (s + 1))
                    a.activation(PTh[:, h, :, tt:2 * tt + 1, :],
                                 two[1][:, 0:NG * (1 + tt) * P]
                                 .rearrange("p (g b q) -> p g b q", g=NG, b=1 + tt), ACT.Copy)\
                        .then_inc(pthi_done, 1)

                def a_hi(h):
                    act.wait_ge(pv_done, hb * 2 + (h // 2 + 1))
                    a.activation(*head_out(hb, h, 0), ACT.Copy).then_inc(ahi_done, 1)

                act.wait_ge(bv_out, 16)
                load_bias(0)
                load_bias(1)
                for j in range(4):
                    hi(n0 + j + 3, i, step)
                soft(0)
                for m in range(7):
                    if m < 6:
                        v_hi(4 + m // 2, m % 2)
                    soft(m + 1)
                    if m in (0, 2):
                        load_bias(m // 2 + 2)
                    p_hi(m)
                    if m:
                        h0 = (m + 1) % 2 * (KD // 2)
                        hi(n0 + 4 + (m - 1) // 2 + 3, i, step, h0, h0 + KD // 2)
                if not last:
                    hi(n0 + 7 + 3, i, step)
                p_hi(7)
                a_hi(0)
                a_hi(1)
                a_hi(2)
                a_hi(3)
                if not last:
                    hi(n0 + 8 + 3, i, step)

            hi(U_QKV + 3)
            root_of(2, S + NT, 7)
            hi(U_QKV + 4)
            act.wait_ge(rstd_done, 3)
            with act.Fori(0, NHB - 1) as i:
                block(i, 9, False)
            block(0, 0, True)
            projected(U_BOUT, 24, ((xsB, V_F1),))
            ffn(1, U_UP1, E_UP1, U_DOWN1, 32, (), 3)
            for k in range(Y_POOL, KD):
                a.activation(Y[:, k, :], X[:, k, :], ACT.Copy, scale=col(V_FIN + k))\
                    .then_inc(yg_done, 1)
            root_of(4, S, 6)

        @block.vector
        def _(dve):
            v = nc.vector

            def lo(n, i=0, step=0, k0=0, k1=KD):
                if n % RING or n >= U_END:
                    return
                dve.wait_ge(hi_done[0], rnd(n, i, step) + 1)
                o = v.tensor_tensor(wlo[0][:, k0:k1, :],
                                    raw[0][:, k0 * CW:k1 * CW].rearrange("p (k c) -> p k c", c=CW),
                                    whi[0][:, k0:k1, :].bitcast(F32), ALU.subtract)
                if k1 == KD:
                    o.then_inc(lo_done[0], 1)

            def acc_clear(q):
                if q:
                    dve.wait_ge(ss_done, q // 8)
                v.memset(acc[:, :], 0.0).then_inc(acc_zero, 1)
                dve.wait_ge(acc_zero, q // 8 + 1)

            def gained(k, x0, sets, i=0, dq=0):
                for m, (dst, gain) in enumerate(sets):
                    dve.wait_ge(xhi_done, x0 + m + 1 + i * (dq * len(sets)))
                    v.scalar_tensor_tensor(dst[:, bass.ds(k, 1), 1, :], X[:, bass.ds(k, 1), :],
                                           vcols[:, bass.ds(k + gain, 1)],
                                           dst[:, bass.ds(k, 1), 0, :].bitcast(F32),
                                           ALU.mult, ALU.subtract).then_inc(xlo_done, 1)

            def added(q, i=0, dq=0):
                dve.wait_ge(sq_done, q + i * dq + 1)
                ge(dve, acc_done, q + i * dq)
                v.tensor_tensor(acc[:, :], acc[:, :], sq[:, q % 2, :], ALU.add)\
                    .then_inc(acc_done, 1)

            def post(k, q, x0, sets, i=0, dq=0):
                gained(k, x0, sets, i, dq)
                added(q, i, dq)

            def gated(k):
                dve.wait_ge(sig_done, k + 1)
                dve.wait_ge(hn_done, k // 2 + 1)
                hk = hm[:, k // 2, k % 2, :]
                v.scalar_tensor_tensor(hk, hk, col(V_HN + k), sig[:, k, :], ALU.mult, ALU.mult)\
                    .then_inc(hg_done, 1)

            def m_lo(k):
                dve.wait_ge(mhi_done, k + 1)
                v.tensor_tensor(xsB[:, k, 1, :], hm[:, k // 2, k % 2, :],
                                xsB[:, k, 0, :].bitcast(F32), ALU.subtract).then_inc(mlo_done, 1)

            def rstd_of(s, width):
                dve.wait_ge(root_done, s + 1)
                v.reciprocal(rstd[:, 0:width], rstd[:, 0:width]).then_inc(rstd_done, 1)
                dve.wait_ge(rstd_done, s + 1)

            def complete(c, m, n, i=0, step=0):
                if c:
                    dve.wait_ge(w_used[n % RING], rnd(n, i, step) + 1)
                else:
                    dve.wait_ge(tile_done, m + 1)

            def residual(k, c, m, n, b, i=0, step=0):
                complete(c, m, n, i, step)
                xk = X[:, bass.ds(k, 1), :].rearrange("p a t -> p (a t)")
                v.tensor_tensor(xk, xk, bank[b][:, 0:S], ALU.add).then_inc(x_new, 1)

            acc_clear(0)
            dve.wait_ge(v_in, 16)
            for half in range(2):
                dve.wait_ge(x_in[half], 16)
                for k in range(4 * half, 4 * half + 4):
                    gained(k, k, ((xsA, V_A),))
                if half == 0:
                    dve.wait_ge(first_hi, 1)
                    v.tensor_tensor(wlo[0][:, 0:4, :], raw[0][:, 0:4 * CW]
                                    .rearrange("p (k c) -> p k c", c=CW),
                                    whi[0][:, 0:4, :].bitcast(F32), ALU.subtract)\
                        .then_inc(first_lo, 1)
            lo(0, k0=4)
            for k in range(4):
                added(k)
            dve.wait_ge(hi_done[1], 1)
            v.tensor_tensor(wlo[1][:, 0:SHARE, :], raw[1][:, 0:SHARE * CW]
                            .rearrange("p (k c) -> p k c", c=CW),
                            whi[1][:, 0:SHARE, :].bitcast(F32), ALU.subtract).then_inc(share_lo, 1)
            for k in range(4, KD):
                added(k)
            rstd_of(0, S + NT)
            dve.wait_ge(wgh_done, 1)
            v.tensor_tensor(wg4[:, :, 2:4, 0:AH], wg[:, :, :].rearrange("p k (j h) -> p k j h", j=2),
                            wg4[:, :, 0:2, 0:AH].bitcast(F32), ALU.subtract).then_inc(wgl_done, 1)
            def head_done(h):
                dve.wait_ge(den_abs, h + 1)
                v.tensor_tensor(den[:, h, :], den[:, h, :], EB[:, h, :], ALU.max)\
                    .then_inc(dmax_done, 1)
                dve.wait_ge(dmax_done, h + 1)
                v.reciprocal(den[:, h, :], den[:, h, :]).then_inc(dinv_done, 1)
                dve.wait_ge(dinv_done, h + 1)
                dve.wait_ge(num_done, h + 1)
                v.tensor_tensor(hm[:, h, :, :],
                                bank[3 + h][:, :].rearrange("p (c t) -> p c t", c=2),
                                den[:, h:h + 1, :].to_broadcast([P, 2, S]), ALU.mult)\
                    .then_inc(hm_done, 1)

            def head_normed(h):
                dve.wait_ge(hroot_done, h // 2 + 1)
                v.reciprocal(hrs[:, h, :], hroot[:, h, :]).then_inc(hrs_done, 1)
                dve.wait_ge(hrs_done, h + 1)
                v.tensor_tensor(hm[:, h, :, :], hm[:, h, :, :],
                                hrs[:, h:h + 1, :].to_broadcast([P, 2, S]), ALU.mult)\
                    .then_inc(hn_done, 1)

            for u in range(12):
                lo(u + 2)
                if u == 2:
                    dve.wait_ge(gates_ps, 1)
                    v.tensor_copy(gtmp[:, :], bank[3][64:P, 0:S]).then_inc(gtmp_done, 1)
                    dve.wait_ge(gtmp_done, 1)
                    v.tensor_tensor(gtmp[:, :], gtmp[:, :], bank[3][0:64, 0:S], ALU.add)\
                        .then_inc(gtmp_done, 1)
                    dve.wait_ge(gtmp_done, 2)
                    for j in range(2):
                        ps = slice(32 * j, 32 * j + AH)
                        v.tensor_tensor(gz[:, j, :], gtmp[ps, :], rstd[ps, 0:S], ALU.mult)\
                            .then_inc(gtmp_done, 1)
                if u == 3:
                    dve.wait_ge(bt_done, 1)
                    v.tensor_copy(bv[:, :], bank[6][0:NG * BH, 0:DIST]).then_inc(bt_copied, 1)
                    dve.wait_ge(gtmp_done, 4)
                    for j in range(2):
                        v.tensor_scalar(gz[:, j, :], gz[:, j, :], bif[:, j:j + 1], None, ALU.add)\
                            .then_inc(gseq, 1)
                    dve.wait_ge(gact, 3)
                    v.tensor_tensor_scan(gn[:, :], gones[:, :], gl[:, :], 0.0, ALU.mult, ALU.add)\
                        .then_inc(gseq, 1)
                    dve.wait_ge(gseq, 3)
                    v.scalar_tensor_tensor(gc[:, :], gt[:, 0, :], CAP, gn[:, :], ALU.mult, ALU.add)\
                        .then_inc(gseq, 1)
                    dve.wait_ge(gseq, 4)
                    v.tensor_tensor_scan(gm[:, :], gc[:, :], gc[:, :], 0.0, ALU.max, ALU.max)\
                        .then_inc(gseq, 1)
                    dve.wait_ge(gseq, 5)
                    v.tensor_tensor(gd[:, :], gn[:, :], gm[:, :], ALU.subtract).then_inc(gseq, 1)
                    dve.wait_ge(gseq, 5)
                    v.tensor_copy(gmx[0:AH, 0, :], gm[:, :]).then_inc(gmx_hi, 1)
                    dve.wait_ge(gmx_hi, 1)
                    v.tensor_tensor(gmx[32:32 + AH, 0, :], gm[:, :], gmx[0:AH, 0, :].bitcast(F32),
                                    ALU.subtract).then_inc(gmx_lo, 1)
                    dve.wait_ge(gates_done, 1)
                    v.tensor_copy(gmx[0:AH, 1, :], gx[:, :]).then_inc(gmx_hi, 1)
                    dve.wait_ge(gmx_hi, 2)
                    v.tensor_tensor(gmx[32:32 + AH, 1, :], gx[:, :], gmx[0:AH, 1, :].bitcast(F32),
                                    ALU.subtract).then_inc(gmx_lo, 1)
                if u == 5:
                    dve.wait_ge(ct_done, 1)
                    v.tensor_copy(cS[:, :, :].rearrange("p s h -> p (s h)"),
                                  bank[4][:, 0:NT * AH]).then_inc(cs_done, 1)
                    dve.wait_ge(cs_done, 1)
                    for h in range(AH):
                        dve.wait_ge(mb_done, 2 * (h // 2) + 2)
                        m = bank[5 + h // 2][:, (h % 2) * S:(h % 2 + 1) * S]
                        v.tensor_scalar(EE[:, h, 0:S], m, cS[:, 0, h:h + 1], 0.0,
                                        ALU.subtract, ALU.max).then_inc(ee_done, 1)
                        v.tensor_scalar(EE[:, h, S:384], m[:, P:S], cS[:, 1, h:h + 1], 0.0,
                                        ALU.subtract, ALU.max).then_inc(ee_done, 1)
                if u == 6:
                    for h in range(AH):
                        dve.wait_ge(s_done, h + 1)
                        dve.wait_ge(dm_done, 2)
                        v.scalar_tensor_tensor(SD[:, h, :], bank[3 + h][:, 0:384], DK ** -0.5,
                                               EE[:, h, :], ALU.mult, ALU.mult)\
                            .then_inc(sd_done, 1)
                if u == 11:
                    for k in range(4):
                        gated(k)
                    for k in range(4):
                        m_lo(k)
                for c in range(2):
                    if (u, c) in ((7, 0), (7, 1), (8, 0), (9, 0)):
                        head_done(((7, 0), (7, 1), (8, 0), (9, 0)).index((u, c)))
                    if (u, c) in ((8, 1), (9, 1), (10, 0), (10, 1)):
                        head_normed(((8, 1), (9, 1), (10, 0), (10, 1)).index((u, c)))
                    t = 2 * u + c
                    complete(c, T_IN + u, U_IN + u)
                    ps = bank[in_bank(t)][:, 0:S]
                    if u < 2:
                        o = v.tensor_tensor(qT[:, 2 * u + c, :], ps, rstd[:, 0:S], ALU.mult)
                    elif u < 4:
                        o = v.tensor_tensor(kT[:, 2 * (u - 2) + c, :], ps, rstd[:, 0:S], ALU.mult)
                    elif u < 8:
                        o = v.tensor_scalar(Vm[:, c, (u - 4) * CW:(u - 3) * CW], ps,
                                            rstd[:, S + c:S + c + 1], None, ALU.mult)
                    else:
                        o = v.tensor_tensor(sig[:, 2 * (u - 8) + c, :], ps, rstd[:, 0:S], ALU.mult)
                    o.then_inc(ev_done, 1)
            for k in (4, 6):
                gated(k)
                gated(k + 1)
                m_lo(k)
                m_lo(k + 1)

            def outproj(u0, t0, q0, x0, sets, banks):
                acc_clear(q0)
                for u in range(4):
                    for c in range(2):
                        residual(2 * u + c, c, t0 + u, u0 + u, banks[u][c])
                    if u == 1:
                        lo(u0 + 3)
                        lo(u0 + 4)
                    for c in range(2):
                        dve.wait_ge(x_new, q0 + 2 * u + c + 1 - KD)
                        post(2 * u + c, q0 + 2 * u + c, x0 + 2 * u + c, sets)

            outproj(U_AOUT, T_AOUT, 8, 8, ((xsA, V_F0),), OB0)

            def ffn(layer, u_up, t_up, u_down, t_down, q0, x0, sets, s):
                f0, p0 = 4 * PAIRS * layer, PAIRS * layer
                def read_out(p, g, n, i, step):
                    for c in range(2):
                        j = 2 * g + c
                        complete(c, p * 2 + (t_up + g), n + g, i, step)
                        ge(dve, cB_done, 4 * p + (f0 - 4 + j + 1))
                        v.tensor_tensor(ub[:, j, 2:S + 2], bank[FB[j]][:, 0:S], rstd[:, 0:S], ALU.mult)\
                            .then_inc(ev_done, 1)

                def taps(p, g):
                    for c in range(2):
                        j = 2 * g + c
                        dve.wait_ge(t1_done, 4 * p + (f0 + j + 1))
                        v.scalar_tensor_tensor(cb[:, j, :], ub[:, j, 1:S + 1],
                                               conv_col(layer, 1, p * 2 + (KF * g + c)),
                                               cb[:, j, :], ALU.mult, ALU.add).then_inc(cA_done, 1)
                    for c in range(2):
                        j = 2 * g + c
                        dve.wait_ge(cA_done, 4 * p + (f0 + j + 1))
                        v.scalar_tensor_tensor(cb[:, j, :], ub[:, j, 0:S],
                                               conv_col(layer, 0, p * 2 + (KF * g + c)),
                                               cb[:, j, :], ALU.mult, ALU.add).then_inc(cB_done, 1)

                def product(p):
                    dve.wait_ge(silu_done, p + (p0 + 1))
                    dve.wait_ge(cB_done, 4 * p + (f0 + 4))
                    v.tensor_tensor(hb_[:, :, :], gb[:, :, :], cb[:, 2:4, :], ALU.mult)\
                        .then_inc(mul_done, 1)

                def h_lo(p):
                    dve.wait_ge(hhi_done, p + (p0 + 1))
                    v.tensor_tensor(hs[:, bass.ds(2 * p, 2), 1, :], hb_[:, :, :],
                                    hs[:, bass.ds(2 * p, 2), 0, :].bitcast(F32), ALU.subtract)\
                        .then_inc(hlo_done, 1)

                def pair(n, p, i, step, first):
                    lo(n + 2, i, step)
                    if first:
                        rstd_of(s, S)
                    read_out(p, 0, n, i, step)
                    if not first:
                        taps(p - 1, 1)
                        product(p - 1)
                    lo(n + 3, i, step)
                    read_out(p, 1, n, i, step)
                    taps(p, 0)
                    if not first:
                        h_lo(p - 1)

                v.memset(ub[:, :, 0:2], 0.0).then_inc(pad_done, 1)
                dve.wait_ge(pad_done, layer + 1)
                pair(u_up, 0, 0, 0, True)
                with dve.Fori(0, 3) as i:
                    for j in range(3):
                        pair(u_up + 2 + 2 * j, i * 3 + (1 + j), i, 6, False)
                pair(u_up + 20, PAIRS - 1, 0, 0, False)
                taps(PAIRS - 1, 1)
                product(PAIRS - 1)
                h_lo(PAIRS - 1)
                acc_clear(q0)

                def column(i, n, ii, step, last):
                    lo(n + 2, ii, step)
                    lo(n + 3, ii, step)
                    m = 6 if last else 0
                    for c in range(2):
                        residual(i * 2 + c, c, i + t_down, n + 2, 4 + c, ii, step)
                    if not last:
                        lo(n + 4, ii, step)
                    for c in range(2):
                        dve.wait_ge(x_new, q0 + m + c + 1 - KD + ii * (0 if last else 2))
                        post(i * 2 + c, q0 + m + c, x0 + (m + c) * len(sets), sets, ii,
                             0 if last else 2)
                    if last:
                        lo(n + 4)

                with dve.Fori(0, 3) as i:
                    column(i, u_down, i, 3, False)
                column(3, u_down + 9, 0, 0, True)

            dve.wait_ge(bv_out, 16)
            ffn(0, U_UP0, T_UP0, U_DOWN0, T_DOWN0, 16, 16, ((xsA, V_KV), (xsB, V_B)), 1)

            def block(i, step, last):
                n0 = U_BODY + (27 if last else 0)
                hb = NHB - 1 if last else i

                def evac(j, c):
                    if j < 7 or not last:
                        read_qkv(n0 + j, i, step, hb * 9 + (2 + j), 2 + j, c, *BODY[j])

                def biased(s):
                    h, tt = divmod(s, 2)
                    w = P * (1 + tt)
                    dve.wait_ge(sc_done, hb * 8 + (s + 1))
                    if tt == 0:
                        dve.wait_ge(bi_in[h], hb * 16 + 16)
                    if s >= 2:
                        dve.wait_ge(tr_done, hb * 8 + (s - 1))
                    v.memset(carry[:, s % 2:s % 2 + 1], 0.0)
                    bb = Bi[:, h % 2, :, :] if tt else Bi[:, h % 2, :, P:S]
                    v.tensor_tensor_reduce(
                        out=SB[:, s % 2, 0:NG * w].rearrange("p (g f) -> p g f", g=NG),
                        in0=two[0][:, 0:NG * w].rearrange("p (g f) -> p g f", g=NG), in1=bb,
                        scale=1.0, scalar=-3e38, op0=ALU.add, op1=ALU.max,
                        accum_out=mxx[:, s:s + 1]).then_inc(smax_done, 1)
                    dve.wait_ge(smax_done, hb * 8 + (s + 1))
                    v.tensor_scalar(nmx[:, s:s + 1], mxx[:, s:s + 1], -1.0, None, ALU.mult)\
                        .then_inc(nmx_done, 1)

                def normed(s):
                    w = NG * P * (1 + s % 2)
                    dve.wait_ge(exp_done, hb * 8 + (s + 1))
                    v.reciprocal(linv[:, s:s + 1], lsum[:, s:s + 1]).then_inc(linv_done, 1)
                    dve.wait_ge(linv_done, hb * 8 + (s + 1))
                    v.tensor_scalar(SB[:, s % 2, 0:w], SB[:, s % 2, 0:w], linv[:, s:s + 1], None,
                                    ALU.mult).then_inc(p_done, 1)

                def p_lo(s):
                    h, tt = divmod(s, 2)
                    dve.wait_ge(pthi_done, hb * 8 + (s + 1))
                    v.tensor_tensor(PTl[:, h, :, tt:2 * tt + 1, :],
                                    two[1][:, 0:NG * (1 + tt) * P]
                                    .rearrange("p (g b q) -> p g b q", g=NG, b=1 + tt),
                                    PTh[:, h, :, tt:2 * tt + 1, :].bitcast(F32), ALU.subtract)\
                        .then_inc(ptlo_done, 1)

                def a_lo(h):
                    dve.wait_ge(ahi_done, hb * HB + (h + 1))
                    dst, src = head_out(hb, h, 1)
                    v.tensor_tensor(dst, src, head_out(hb, h, 0)[0].bitcast(F32), ALU.subtract)\
                        .then_inc(alo_done, 1)

                for j in range(4):
                    lo(n0 + j + 2, i, step)
                    evac(j, 0)
                    evac(j, 1)
                biased(0)
                for m in range(7):
                    normed(m)
                    biased(m + 1)
                    if m:
                        h0 = (m + 1) % 2 * (KD // 2)
                        lo(n0 + 4 + (m - 1) // 2 + 2, i, step, h0, h0 + KD // 2)
                    evac(4 + m // 2, m % 2)
                    p_lo(m)
                normed(7)
                evac(7, 1)
                p_lo(7)
                a_lo(0)
                a_lo(1)
                evac(8, 0)
                a_lo(2)
                a_lo(3)
                evac(8, 1)

            def read_qkv(n, i, step, m, u, c, kind, g):
                complete(c, m + T_QKV, n, i, step)
                ps = bank[qkv_bank(u, c, n < U_BODY)][:, 0:S]
                if kind == "q":
                    o = v.scalar_tensor_tensor(
                        QT[:, g, c, :].rearrange("p (a t) -> p a t", a=NT)[:, :, ::-1],
                        ps.rearrange("p (a t) -> p a t", a=NT), DH ** -0.5,
                        rstd[:, 0:S].rearrange("p (a t) -> p a t", a=NT), ALU.mult, ALU.mult)
                elif kind == "k":
                    o = v.tensor_tensor(KT[:, g, c, :], ps, rstd[:, 0:S], ALU.mult)
                else:
                    dve.wait_ge(vhi_done, (n_v(n) + c + 1) + (i * 6 if step else 0))
                    o = v.scalar_tensor_tensor(Vl[:, c, g, :], ps, rstd[:, S + c:S + c + 1],
                                               Vh[:, c, g, :].bitcast(F32), ALU.mult, ALU.subtract)
                o.then_inc(ev_done, 1)

            lo(U_QKV + 2)
            rstd_of(2, S + NT)
            for u in range(2):
                if u:
                    lo(U_QKV + u + 2)
                for c in range(2):
                    read_qkv(U_QKV + u, 0, 0, u, u, c, "qk"[u], 0)
            with dve.Fori(0, NHB - 1) as i:
                block(i, 9, False)
            block(0, 0, True)
            outproj(U_BOUT, T_BOUT, 24, 32, ((xsB, V_F1),), OB1)
            ffn(1, U_UP1, T_UP1, U_DOWN1, T_DOWN1, 32, 40, (), 3)

            rstd_of(4, S)
            for k in range(Y_POOL):
                v.scalar_tensor_tensor(Y[:, k, :], X[:, k, :], col(V_FIN + k), rstd[:, 0:S],
                                       ALU.mult, ALU.mult).then_inc(yn_done, 1)

        @block.tensor
        def _(pe):
            t_ = nc.tensor

            def three(ps, hi_w, lo_w, hi_x, lo_x, first, last):
                t_.matmul(ps, hi_w, hi_x, start=first, stop=False)
                t_.matmul(ps, hi_w, lo_x, start=False, stop=False)
                return t_.matmul(ps, lo_w, hi_x, start=False, stop=last)

            def unit(n, xs, banks, i=0, step=0, ks=(0, KD), ktot=KD, wait_bank=(), k_wait=None, part=None,
                     token_major=False):
                s = n % RING
                if n:
                    pe.wait_ge(lo_done[s], rnd(n, i, step) + 1)
                k0, k1 = ks
                order = [(k, c) for k in range(k0, k1) for c in range(2)] if k_wait else \
                    [(k, c) for c in range(2) for k in range(k0, k1)]
                if part:
                    order = [(k, c) for k, c in order if part[0] <= k < part[1]]
                for k, c in order:
                    if k_wait and c == 0:
                        k_wait(k)
                    if k == k0 and c < len(wait_bank) and wait_bank[c] is not None:
                        ge(pe, *wait_bank[c])
                    cs = slice(c * P, (c + 1) * P)
                    first, last = k == 0, k == ktot - 1
                    kk = k - k0
                    if token_major:
                        ps = bank[banks[c]][:, 0:CW]
                        t_.matmul(ps, xs[:, k, 0, cs], whi[s][:, kk, :], start=first, stop=False)
                        t_.matmul(ps, xs[:, k, 0, cs], wlo[s][:, kk, :], start=False, stop=False)
                        mm = t_.matmul(ps, xs[:, k, 1, cs], whi[s][:, kk, :], start=False,
                                       stop=last)
                    else:
                        mm = three(bank[banks[c]][:, 0:S], whi[s][:, kk, cs], wlo[s][:, kk, cs],
                                   xs[:, k, 0, :], xs[:, k, 1, :], first, last)
                    if (k, c) == order[-1] and k == k1 - 1:
                        mm.then_inc(w_used[s], 1)
                    elif last:
                        mm.then_inc(tile_done, 1)

            def sums(s, b, tokens):
                pe.wait_ge(acc_done, 8 * (s + 1))
                mm = t_.matmul(bank[b][:, 0:S], ones[:], acc[:, :], start=True, stop=True)
                if tokens:
                    for tt in range(NT):
                        mm = t_.matmul(bank[b][:, S + tt:S + tt + 1], acc[:, tt * P:(tt + 1) * P],
                                       ones[:, 0:1], start=True, stop=True)
                mm.then_inc(ss_done, 1)

            def first_wait(k):
                pe.wait_ge(xlo_done, k + 1)
                if k == 0:
                    pe.wait_ge(first_lo, 1)
                elif k == 4:
                    pe.wait_ge(lo_done[0], 1)

            for u in range(12):
                t = 2 * u
                if u == 1:
                    pe.wait_ge(share_lo, 1)
                waits = [(ev_done, t + c - 2) for c in range(2)]
                if u == 1:
                    unit(U_IN + 1, xsA, [in_bank(2), in_bank(3)], part=(0, 2))
                    pe.wait_ge(consts, 12)
                    sums(0, 7, True)
                unit(U_IN + u, xsA, [in_bank(t), in_bank(t + 1)],
                     wait_bank=() if u == 1 else waits, part=(2, KD) if u == 1 else None,
                     k_wait=None if u else first_wait,
                     token_major=4 <= u < 8)
                if u == 1:
                    pe.wait_ge(wgl_done, 1)
                    for k in range(KD):
                        for part in range(2):
                            mm = t_.matmul(bank[3][:, 0:S],
                                           wg4[:, k, :, :].rearrange("p j c -> p (j c)"),
                                           xsA[:, k, part, :], start=k == part == 0,
                                           stop=k == KD - 1 and part == 1)
                    mm.then_inc(gates_ps, 1)
                if u == 2:
                    pe.wait_ge(c_in, 64)
                    t_.matmul(bank[6][0:NG * BH, 0:DIST], rb[:, :], oh[:, :], start=True,
                              stop=False)
                    t_.matmul(bank[6][0:NG * BH, 0:DIST], gs[:, :], mk[:, :], start=False,
                              stop=True).then_inc(bt_done, 1)
                if u == 4:
                    pe.wait_ge(gmx_lo, 2)
                    for st in range(NT):
                        mm = t_.transpose(bank[4][:, st * AH:(st + 1) * AH],
                                          gc[:, st * P:(st + 1) * P], ident[0:AH, 0:AH])
                    mm.then_inc(ct_done, 1)
                    for h in range(AH):
                        t_.matmul(bank[5 + h // 2][:, (h % 2) * S:(h % 2 + 1) * S], selr[:, h, :],
                                  gmx[:, 0, :], start=True, stop=True).then_inc(mb_done, 1)
                    for h in range(AH):
                        mm = t_.matmul(bank[(3, 7)[h // 2]][:, (h % 2) * S:(h % 2 + 1) * S],
                                       selr[:, h, :], gmx[:, 1, :], start=True, stop=True)
                        if h % 2:
                            mm.then_inc(eb_done, 1)
                if u == 5:
                    pe.wait_ge(ev_done, 8)
                    pe.wait_ge(ee_done, 2 * AH)
                    pe.wait_ge(eb_copied, 2)
                    for h in range(AH):
                        b = bank[3 + h]
                        t_.matmul(b[:, 0:S], kT[:, h, 0:P], qT[:, h, :], start=True, stop=True)
                        t_.matmul(b[:, S:384], kT[:, h, P:S], qT[:, h, P:S], start=True, stop=True)\
                            .then_inc(s_done, 1)
                for h in {6: (0, 1), 7: (2,), 8: (3,)}.get(u, ()):
                    b = bank[3 + h]
                    pe.wait_ge(ev_done, 2 * (4 + h) + 2)
                    pe.wait_ge(sd_done, h + 1)
                    ge(pe, den_abs, h)
                    t_.matmul(bank[7][:, 0:S], ones[:], SD[:, h, 0:S], start=True, stop=False)
                    t_.matmul(bank[7][:, P:S], ones[:], SD[:, h, S:384], start=False, stop=True)\
                        .then_inc(den_done, 1)
                    for c in range(2):
                        cs = slice(h * DV + c * P, h * DV + (c + 1) * P)
                        t_.matmul(b[:, c * S:(c + 1) * S], Vm[:, 0, cs], SD[:, h, 0:S],
                                  start=True, stop=False)
                        mm = t_.matmul(b[:, c * S + P:(c + 1) * S], Vm[:, 1, cs],
                                       SD[:, h, S:384], start=False, stop=True)
                    mm.then_inc(num_done, 1)
                if u in (7, 9):
                    for h in (0, 1) if u == 7 else (2, 3):
                        pe.wait_ge(hsq_done, h + 1)
                        ps = bank[3 + h // 2][:, (h % 2) * S:(h % 2 + 1) * S]
                        t_.matmul(ps, ones[:], hsq[:, h, 0, :], start=True, stop=False)
                        mm = t_.matmul(ps, ones[:], hsq[:, h, 1, :], start=False, stop=True)
                        if h % 2:
                            mm.then_inc(hss_done, 1)

            def outproj(u0, e0, xs, k_wait, q0, banks, begun):
                if not begun:
                    unit(u0, xs, banks[0], k_wait=k_wait, part=(0, HEAD_K))
                pe.wait_ge(ev_done, e0)
                unit(u0 + 1, xs, banks[1], part=(0, HEAD_K))
                unit(u0, xs, banks[0], k_wait=k_wait, part=(HEAD_K, KD))
                unit(u0 + 1, xs, banks[1], part=(HEAD_K, KD))
                unit(u0 + 2, xs, banks[2])
                unit(u0 + 3, xs, banks[3], wait_bank=[(x_new, q0 - KD + c + 1) for c in range(2)])

            def ffn(u_up, e_up, u_down, p0, xs, x0, q0, s):
                def pair(n, p, i, step, first):
                    for g in range(2):
                        if first:
                            waits = [(x_new, q0 - KD - 3 + 2 * g + c) for c in range(2)]
                        else:
                            waits = [(ev_done, 4 * p + (e_up - 4 + 2 * g + c + 1)) for c in range(2)]
                        unit(n + g, xs, FB[2 * g:2 * g + 2], i, step, wait_bank=waits,
                             k_wait=(lambda k: pe.wait_ge(xlo_done, x0 + k + 1))
                             if first and not g else None)
                        if first and not g:
                            sums(s, 6, False)

                pair(u_up, 0, 0, 0, True)
                with pe.Fori(0, 3) as i:
                    for j in range(3):
                        pair(u_up + 2 + 2 * j, i * 3 + (1 + j), i, 6, False)
                pair(u_up + 20, PAIRS - 1, 0, 0, False)
                with pe.Fori(0, 4) as i:
                    for j, ks in enumerate(DOWN_K):
                        pe.wait_ge(hlo_done, p0 + ks[1] // 2)
                        unit(u_down + j, hs, [4, 5], i, 3, ks, KF,
                             wait_bank=[(x_new, i * 2 + (q0 - KD + c - 1)) for c in range(2)]
                             if j == 0 else ())

            outproj(U_AOUT, E_UP0, xsB, lambda k: pe.wait_ge(mlo_done, k + 1), 8, OB0, False)
            ffn(U_UP0, E_UP0, U_DOWN0, 0, xsA, 8, 16, 1)

            def tile_of(n, i, step, ev, u, c, kind, k_wait=None, midway=None):
                s = n % RING
                if c == 0:
                    pe.wait_ge(lo_done[s], rnd(n, i, step) + 1)
                if n != U_QKV + 1:
                    pe.wait_ge(ev_done, ev + (c - 2))
                ps = bank[qkv_bank(u, c, n < U_BODY)][:, 0:CW]
                cs = slice(c * P, (c + 1) * P)
                xs = xsB if kind == "q" else xsA
                for k in range(KD):
                    if k_wait and c == 0:
                        k_wait(k)
                    if midway and k == KD // 2:
                        midway()
                    first, last = k == 0, k == KD - 1
                    if kind == "v":
                        t_.matmul(ps, xs[:, k, 0, cs], whi[s][:, k, :], start=first, stop=False)
                        t_.matmul(ps, xs[:, k, 0, cs], wlo[s][:, k, :], start=False, stop=False)
                        mm = t_.matmul(ps, xs[:, k, 1, cs], whi[s][:, k, :], start=False, stop=last)
                    else:
                        mm = three(ps, whi[s][:, k, cs], wlo[s][:, k, cs], xs[:, k, 0, :],
                                   xs[:, k, 1, :], first, last)
                mm.then_inc(w_used[s] if c else tile_done, 1)

            def block(i, step, last):
                n0 = U_BODY + (27 if last else 0)
                hb = NHB - 1 if last else i

                def tile(j, c, midway=None):
                    if j < 7 or not last:
                        tile_of(n0 + j, i, step, hb * 18 + (E_QKV + 2 * (2 + j)), 2 + j, c,
                                BODY[j][0], midway=midway)
                    elif midway:
                        midway()

                def scores(s):
                    h, tt = divmod(s, 2)
                    rows = slice((h % 2) * DH, (h % 2 + 1) * DH)
                    w = P * (1 + tt)
                    if s == 0:
                        pe.wait_ge(ev_done, hb * 18 + (E_QKV + 12))
                    else:
                        pe.wait_ge(smax_done, hb * 8 + s)
                    for g in range(NG):
                        mm = t_.matmul(two[0][:, g * w:(g + 1) * w],
                                       QT[rows, g, h // 2, tt * P:(tt + 1) * P],
                                       KT[rows, g, h // 2, 0:w], start=True, stop=True)
                    mm.then_inc(sc_done, 1)

                def turned(s):
                    tt = s % 2
                    pe.wait_ge(p_done, hb * 8 + (s + 1))
                    if s:
                        pe.wait_ge(ptlo_done, hb * 8 + s)
                    for b in range(NG * (1 + tt)):
                        mm = t_.transpose(two[1][:, b * P:(b + 1) * P],
                                          SB[:, s % 2, b * P:(b + 1) * P], ident[:])
                    mm.then_inc(tr_done, 1)

                def mixed(c, midway=None):
                    pe.wait_ge(ptlo_done, hb * 8 + (4 * c + 4))
                    if c == 0:
                        pe.wait_ge(ev_done, hb * 18 + (E_QKV + 18))
                    else:
                        pe.wait_ge(smax_done, hb * 8 + 8)
                    ps = bank[(7, 4)[c]][:, :].rearrange("p (h t) -> p h t", h=2)
                    cs = slice(c * P, (c + 1) * P)
                    for g in range(NG):
                        if midway and g == 1:
                            midway()
                        for kt in range(NT):
                            ph, pl = (x[:, 2 * c:2 * c + 2, g, 2 * kt:2 + kt, :]
                                      .rearrange("p h b q -> p h (b q)") for x in (PTh, PTl))
                            mm = three(ps[:, :, kt * P:S], Vh[:, kt, g, cs], Vl[:, kt, g, cs],
                                       ph, pl, g == kt == 0, g == NG - 1 and kt == 1)
                    mm.then_inc(pv_done, 1)

                def projected(k0, k1, midway=None):
                    s = U_BOUT % RING
                    pe.wait_ge(lo_done[s], rnd(U_BOUT) + 1)
                    pe.wait_ge(alo_done, HB * (NHB - 1))
                    pe.wait_ge(ev_done, E_UP1)
                    for k in range(k0, k1):
                        if midway and k == k0 + 2:
                            midway()
                        for c in range(2):
                            cs = slice(c * P, (c + 1) * P)
                            three(bank[c][:, 0:S], whi[s][:, k, cs], wlo[s][:, k, cs],
                                  aTs[:, k, 0, :], aTs[:, k, 1, :], k == 0, False)

                for j in range(4):
                    tile(j, 0)
                    tile(j, 1)
                for m in range(7):
                    tile(4 + m // 2, m % 2, lambda: turned(m - 1) if m else scores(0))
                    scores(m + 1)
                if last:
                    projected(0, 5, lambda: turned(6))
                else:
                    tile(7, 1, lambda: turned(6))
                mixed(0, lambda: turned(7))
                if last:
                    projected(5, HEAD_K)
                else:
                    tile(8, 0)
                mixed(1)
                tile(8, 1)

            for u in range(2):
                for c in range(2):
                    tile_of(U_QKV + u, 0, 0, E_QKV + 2 * u, u, c, "qk"[u],
                            (lambda k: pe.wait_ge(xlo_done, 16 + 2 * k + 2)) if u == 0 else None)
                if u == 0:
                    sums(2, 7, True)
            with pe.Fori(0, NHB - 1) as i:
                block(i, 9, False)
            block(0, 0, True)

            outproj(U_BOUT, E_UP1, aTs, lambda k: pe.wait_ge(alo_done, 2 * k + 2), 24,
                    OB1, True)
            ffn(U_UP1, E_UP1, U_DOWN1, PAIRS, xsB, 32, 32, 3)
            sums(4, 6, False)


def laid_out(inputs):
    def cols(a):
        return np.asarray(a).reshape(-1, P).T

    g = {n: np.asarray(a) for n, a in inputs.items()}
    vectors = [g["a_norm_g"], g["kv_norm_g"], g["b_norm_g"], g["f_norm_g"][0], g["f_norm_g"][1],
               g["final_norm_g"], g["a_hnorm_g"]]
    for layer in range(2):
        vectors += [g["f_conv_w"][layer, j] for j in range(3)] + [g["f_conv_b"][layer]]
    arrays = {
        "xT": g["x"][0].reshape(S, KD, P).transpose(2, 1, 0),
        "vectors": np.concatenate([cols(v) for v in vectors], axis=1),
        "b_if": g["a_b_if"][0].reshape(2, AH).T,
    }
    for n in ("a_w_in", "a_w_out", "w_kv", "b_w_q", "b_w_out", "rel_bias", "f_w_up", "f_w_down"):
        arrays[n] = g[n]
    arrays.update(zip(("onehot", "mask", "group"), distance_tables()))
    return {n: np.ascontiguousarray(a) for n, a in arrays.items()}


def kernel(**inputs):
    import concourse.bacc as bacc
    from concourse.bass_utils import run_bass_kernel_spmd

    nc = bacc.Bacc("TRN2", target_bir_lowering=False, num_devices=1)
    arrays = laid_out(inputs)
    args = [nc.dram_tensor(f"in_{n}", a.shape, mybir.dt.from_np(a.dtype), kind="ExternalInput").ap()
            for n, a in arrays.items()]
    out = nc.dram_tensor("out", (P, KD, S), F32, kind="ExternalOutput").ap()
    build(nc, *args, out)
    r = run_bass_kernel_spmd(nc, [{f"in_{n}": a for n, a in arrays.items()}], core_ids=[0])
    return np.ascontiguousarray(r.results[0]["out"].transpose(2, 1, 0).reshape(1, S, D))
```
